# Optimizing a Trainium2 kernel written in Bass

```python
import jax, jax.numpy as jnp
from jax import lax
import numpy as np

D_MODEL = 1024
BATCH = 1
SEQ = 2048
DEPTH = 1

GRID_W = 64
CTX_LEN = 256
FOURIER_WIDTH = D_MODEL // 2
FOURIER_GROUPS = 4
FOURIER_GROUP_DIM = FOURIER_WIDTH // FOURIER_GROUPS
HGRN_WIDTH = D_MODEL // 2
HGRN_HEAD_DIM = 128
HGRN_HEADS = HGRN_WIDTH // HGRN_HEAD_DIM
CHUNK = 64
N_BRANCHES = 2
D_FF = 4 * D_MODEL
N_MOD = 6
POS_BASE = 10000.0
LN_EPS = 1e-5
RMS_EPS = 1e-6
DEEPNORM_ALPHA = (2.0 * DEPTH) ** 0.25
DEEPNORM_BETA = (8.0 * DEPTH) ** -0.25
PROJ_SPLITS = (FOURIER_WIDTH, FOURIER_WIDTH + HGRN_WIDTH, FOURIER_WIDTH + 2 * HGRN_WIDTH,
               FOURIER_WIDTH + 3 * HGRN_WIDTH, FOURIER_WIDTH + 4 * HGRN_WIDTH, FOURIER_WIDTH + 5 * HGRN_WIDTH)
PROJ_WIDTH = FOURIER_WIDTH + 5 * HGRN_WIDTH + N_BRANCHES * D_MODEL

kernel_name = 'hybrid_fnet_hgrn2_adaln_deepnorm_block'

def _layernorm(x, g, b):
    xf = x.astype(jnp.float32)
    mu = jnp.mean(xf, axis=-1, keepdims=True)
    var = jnp.mean(jnp.square(xf - mu), axis=-1, keepdims=True)
    return ((xf - mu) * lax.rsqrt(var + LN_EPS) * g + b).astype(x.dtype)

def _modulate(x, shift, scale):
    return x * (1 + scale) + shift

def _sincos_2d(rows, cols, dim):
    quarter = dim // 4
    omega = 1.0 / (POS_BASE ** (jnp.arange(quarter, dtype=jnp.float32) / quarter))
    r = jnp.arange(rows, dtype=jnp.float32)[:, None] * omega
    cc = jnp.arange(cols, dtype=jnp.float32)[:, None] * omega
    er = jnp.concatenate([jnp.sin(r), jnp.cos(r)], axis=-1)
    ec = jnp.concatenate([jnp.sin(cc), jnp.cos(cc)], axis=-1)
    emb = jnp.concatenate([jnp.broadcast_to(er[:, None, :], (rows, cols, dim // 2)),
                           jnp.broadcast_to(ec[None, :, :], (rows, cols, dim // 2))], axis=-1)
    return emb.reshape(rows * cols, dim)

def _lower_bounds(logits):
    p = jax.nn.softmax(logits.astype(jnp.float32), axis=1)
    return jnp.cumsum(p, axis=1)[:, :DEPTH]

def _split_heads(t):
    B, T, _ = t.shape
    return t.reshape(B, T, HGRN_HEADS, HGRN_HEAD_DIM).transpose(0, 2, 1, 3)

def _chunk_scan(q, k, v, log_f, s0):
    B, H, T, DK = q.shape
    DV = v.shape[-1]
    n = T // CHUNK

    def to_chunks(t):
        return jnp.moveaxis(t.astype(jnp.float32).reshape(B, H, n, CHUNK, t.shape[-1]), 2, 0)

    mask = jnp.tril(jnp.ones((CHUNK, CHUNK), dtype=bool))[:, :, None]

    def step(S, inp):
        qc, kc, vc, gc = inp
        b = jnp.cumsum(gc, axis=2)
        o_inter = jnp.einsum('bhtk,bhkv->bhtv', qc * jnp.exp(b), S)
        rel = b[:, :, :, None, :] - b[:, :, None, :, :]
        decay = jnp.where(mask, jnp.exp(jnp.minimum(rel, 0.0)), 0.0)
        scores = jnp.einsum('bhtk,bhsk,bhtsk->bhts', qc, kc, decay)
        o_intra = jnp.einsum('bhts,bhsv->bhtv', scores, vc)
        b_last = b[:, :, -1:, :]
        S_new = (jnp.exp(b_last[:, :, 0, :])[..., None] * S
                 + jnp.einsum('bhsk,bhsv->bhkv', kc * jnp.exp(b_last - b), vc))
        return S_new, o_inter + o_intra

    S_T, o = lax.scan(step, s0, (to_chunks(q), to_chunks(k), to_chunks(v), to_chunks(log_f)))
    o = jnp.moveaxis(o, 0, 2).reshape(B, H, T, DV)
    return o.astype(v.dtype), S_T

def _hgrn_direction(q, v, f_pre, lb, s0):
    lb = lb.reshape(HGRN_HEADS, 1, HGRN_HEAD_DIM)
    f = lb + (1.0 - lb) * jax.nn.sigmoid(f_pre.astype(jnp.float32))
    return _chunk_scan(q, 1.0 - f, v, jnp.log(f), s0)

def _hgrn_branch(q, v, f_fwd, f_bwd, og, norm_g, lb_fwd, lb_bwd, s0_fwd, s0_bwd):
    qh = _split_heads(jax.nn.silu(q))
    vh = _split_heads(v)
    o_f, s_f = _hgrn_direction(qh, vh, _split_heads(f_fwd), lb_fwd, s0_fwd)
    o_b, s_b = _hgrn_direction(qh[:, :, ::-1], vh[:, :, ::-1], _split_heads(f_bwd)[:, :, ::-1], lb_bwd, s0_bwd)
    o = (o_f + o_b[:, :, ::-1]).astype(jnp.float32)
    o = o * lax.rsqrt(jnp.mean(jnp.square(o), axis=-1, keepdims=True) + RMS_EPS)
    B, H, T, dh = o.shape
    o = (o.transpose(0, 2, 1, 3).reshape(B, T, H * dh) * norm_g).astype(q.dtype)
    return o * jax.nn.silu(og), s_f, s_b

def _fourier_mix(u):
    B, T, _ = u.shape
    ug = u.astype(jnp.float32).reshape(B, T, FOURIER_GROUPS, FOURIER_GROUP_DIM)
    y = jnp.fft.fft2(ug, axes=(1, 3), norm='ortho').real
    return y.reshape(B, T, FOURIER_WIDTH).astype(u.dtype)

def _merge(u_four, o_hgrn, gate_pre, w_fp, w_hp, w_o, b_o):
    g_four, g_hgrn = jnp.split(jax.nn.sigmoid(gate_pre.astype(jnp.float32)).astype(u_four.dtype), N_BRANCHES, axis=-1)
    y = g_four * (_fourier_mix(u_four) @ w_fp) + g_hgrn * (o_hgrn @ w_hp)
    return y @ w_o + b_o

def _mlp(h, w1, b1, w2, b2):
    return jnp.square(jax.nn.relu(h @ w1 + b1)) @ w2 + b2

def setup_inputs(seed: int = 0) -> dict:
    key = jax.random.key(seed)
    ks = jax.random.split(key, 24)
    f32 = jnp.float32
    D = D_MODEL
    nrm = lambda k, shape, s: jax.random.normal(k, shape, f32) * s
    w_in = nrm(ks[4], (DEPTH, D, PROJ_WIDTH), D ** -0.5)
    v_lo, v_hi = PROJ_SPLITS[1], PROJ_SPLITS[2]
    w_in = w_in.at[:, :, v_lo:v_hi].multiply(DEEPNORM_BETA)
    return {
        'x': nrm(ks[0], (BATCH, SEQ, D), 1.0),
        'c': nrm(ks[1], (BATCH, D), 1.0),
        'ctx': nrm(ks[2], (BATCH, CTX_LEN, D), 1.0),
        'c_ctx': nrm(ks[3], (D,), 1.0),
        'ln_in_g': 1.0 + nrm(ks[5], (D,), 0.02),
        'ln_in_b': nrm(ks[6], (D,), 0.02),
        'w_ada': nrm(ks[7], (DEPTH, D, N_MOD * D), D ** -0.5),
        'b_ada': nrm(ks[8], (DEPTH, N_MOD * D), 0.02),
        'w_in': w_in,
        'b_in': nrm(ks[9], (DEPTH, PROJ_WIDTH), 0.02),
        'hgrn_lb_logits': nrm(ks[10], (2, DEPTH + 1, HGRN_WIDTH), 0.5),
        'hgrn_norm_g': 1.0 + nrm(ks[11], (DEPTH, HGRN_WIDTH), 0.02),
        'w_four_proj': nrm(ks[12], (DEPTH, FOURIER_WIDTH, D), FOURIER_WIDTH ** -0.5 * DEEPNORM_BETA),
        'w_hgrn_proj': nrm(ks[13], (DEPTH, HGRN_WIDTH, D), HGRN_WIDTH ** -0.5 * DEEPNORM_BETA),
        'w_out': nrm(ks[14], (DEPTH, D, D), D ** -0.5 * DEEPNORM_BETA),
        'b_out': nrm(ks[15], (DEPTH, D), 0.02),
        'w_mlp1': nrm(ks[16], (DEPTH, D, D_FF), D ** -0.5 * DEEPNORM_BETA),
        'b_mlp1': nrm(ks[17], (DEPTH, D_FF), 0.02),
        'w_mlp2': nrm(ks[18], (DEPTH, D_FF, D), D_FF ** -0.5 * DEEPNORM_BETA),
        'b_mlp2': nrm(ks[19], (DEPTH, D), 0.02),
        'ln_post_g': 1.0 + nrm(ks[20], (DEPTH, 2, D), 0.02),
        'ln_post_b': nrm(ks[21], (DEPTH, 2, D), 0.02),
    }

def reference(x, c, ctx, c_ctx, ln_in_g, ln_in_b, w_ada, b_ada, w_in, b_in, hgrn_lb_logits, hgrn_norm_g,
              w_four_proj, w_hgrn_proj, w_out, b_out, w_mlp1, b_mlp1, w_mlp2, b_mlp2, ln_post_g, ln_post_b):
    B, T, D = x.shape
    rows = T // GRID_W
    pos = _sincos_2d(rows, GRID_W, D).astype(x.dtype)
    xl = _layernorm(x + pos[None], ln_in_g, ln_in_b)
    xc = _layernorm(ctx, ln_in_g, ln_in_b)
    lbs = _lower_bounds(hgrn_lb_logits)
    s_zero = jnp.zeros((B, HGRN_HEADS, HGRN_HEAD_DIM, HGRN_HEAD_DIM), jnp.float32)

    for l in range(DEPTH):
        mod_l = jnp.split((jax.nn.silu(c) @ w_ada[l] + b_ada[l])[:, None, :], N_MOD, axis=-1)
        mod_c = jnp.split(jax.nn.silu(c_ctx) @ w_ada[l] + b_ada[l], N_MOD, axis=-1)
        lb_f, lb_b = lbs[0, l], lbs[1, l]

        hc = _modulate(xc, mod_c[0], mod_c[1])
        pc = jnp.split(hc @ w_in[l] + b_in[l], PROJ_SPLITS, axis=-1)
        oc_h, s_f, s_b = _hgrn_branch(pc[1], pc[2], pc[3], pc[4], pc[5], hgrn_norm_g[l], lb_f, lb_b, s_zero, s_zero)
        if l < DEPTH - 1:
            mix_c = _merge(pc[0], oc_h, pc[6], w_four_proj[l], w_hgrn_proj[l], w_out[l], b_out[l])
            xc = _layernorm(DEEPNORM_ALPHA * xc + mod_c[2] * mix_c, ln_post_g[l, 0], ln_post_b[l, 0])
            hc2 = _modulate(xc, mod_c[3], mod_c[4])
            xc = _layernorm(DEEPNORM_ALPHA * xc + mod_c[5] * _mlp(hc2, w_mlp1[l], b_mlp1[l], w_mlp2[l], b_mlp2[l]),
                            ln_post_g[l, 1], ln_post_b[l, 1])

        hl = _modulate(xl, mod_l[0], mod_l[1])
        pl = jnp.split(hl @ w_in[l] + b_in[l], PROJ_SPLITS, axis=-1)
        ol_h, _, _ = _hgrn_branch(pl[1], pl[2], pl[3], pl[4], pl[5], hgrn_norm_g[l], lb_f, lb_b, s_f, s_b)
        mix_l = _merge(pl[0], ol_h, pl[6], w_four_proj[l], w_hgrn_proj[l], w_out[l], b_out[l])
        xl = _layernorm(DEEPNORM_ALPHA * xl + mod_l[2] * mix_l, ln_post_g[l, 0], ln_post_b[l, 0])
        hl2 = _modulate(xl, mod_l[3], mod_l[4])
        xl = _layernorm(DEEPNORM_ALPHA * xl + mod_l[5] * _mlp(hl2, w_mlp1[l], b_mlp1[l], w_mlp2[l], b_mlp2[l]),
                        ln_post_g[l, 1], ln_post_b[l, 1])
    return xl


_drawn_inputs = setup_inputs


def setup_inputs(seed=0):
    import zlib

    import numpy as np

    out = dict(_drawn_inputs(seed))
    spreads = {}
    factors = {'ctx': 21.72,
     'c_ctx': 8.0,
     'ln_in_g': 2.695,
     'ln_in_b': 2.709,
     'b_ada': 5.389,
     'b_in': 8.0,
     'hgrn_lb_logits': 8.0,
     'hgrn_norm_g': 34.399,
     'b_out': 18.109,
     'b_mlp1': 8.0,
     'b_mlp2': 5.418}
    for name, (base, spread) in spreads.items():
        noise = np.random.default_rng([zlib.crc32(name.encode()), seed]).standard_normal(out[name].shape)
        drawn = base * np.exp(spread * noise) if base else spread * noise
        out[name] = __import__('jax').numpy.asarray(drawn.astype(out[name].dtype))
    for name, factor in factors.items():
        out[name] = (out[name] * factor).astype(out[name].dtype)
    return out
```

```python
from contextlib import ExitStack, contextmanager

import numpy as np
import concourse.bass as bass
from concourse import mybir

F32 = mybir.dt.float32
F32R = mybir.dt.float32r
I32 = mybir.dt.int32
ALU = mybir.AluOpType
ACT = mybir.ActivationFunctionType

P = 128
D = 1024
T = 2048
TC = 256
BR = D // 2
H = BR // P
FF = 4 * D
KD = D // P
KB = BR // P
GRID_W = 64
NTT = T // P
LEVELS = [1, 2, 4, 8, 16, 32, 64]
NL = len(LEVELS)
ALPHA = 2.0 ** 0.25
LN_EPS = 1e-5
RMS_EPS = 1e-6
C_U, C_Q, C_V, C_FF, C_FB, C_OG, C_G = 0, BR, 2 * BR, 3 * BR, 4 * BR, 5 * BR, 6 * BR
R_F, R_Q, R_OG, R_G = 0, 2 * BR, 3 * BR, 4 * BR


class Count:

    def __init__(self, sem, credits=0):
        self.sem, self.n, self.moving = sem, credits, 0

    def up(self, ins, by=1):
        ins.then_inc(self.sem, by)
        self.n += by
        return ins

    def wait(self, eng, back=0):
        eng.wait_ge(self.sem, self.moving + (self.n - back))


@contextmanager
def repeat(eng, lo, hi, per):
    at = {c: c.n for c in per}
    with eng.Fori(lo, hi) as i:
        for c, k in per.items():
            c.moving = (i - lo) * k if lo else i * k
        yield i
    for c, k in per.items():
        assert c.n == at[c] + k, (c.sem, c.n, at[c], k)
        c.moving = 0
        c.n = at[c] + k * (hi - lo)


def settle(eng, g):
    eng.sem_inc(g["settled"], 1)


def prime(pool, d, g, sems):
    for sem in sems:
        pool.dma_start(d["pad"][g["primed"]], g["ident"][0:1, 0:16]).then_inc(sem, 16)
        g["primed"] += 1


class Box:

    def __init__(self, nc, name):
        self.nc, self.name, self.ctx, self.nums = nc, name, ExitStack(), []

    def __enter__(self):
        self.ctx.__enter__()
        return self

    def __exit__(self, *a):
        done = self.ctx.__exit__(*a)
        if self.nums and a[0] is None:
            nums = sorted(self.nums)
            with self.nc.Block() as block:
                @block.gpsimd
                def _(pool):
                    first = nums[0]
                    for n, after in zip(nums, nums[1:] + [None]):
                        if after != n + 1:
                            pool.sem_clear(range(first, n + 1))
                            first = after
        return done

    def sb(self, name, shape, dt=F32):
        return self.ctx.enter_context(self.nc.sbuf_tensor(f"{self.name}_{name}", shape, dt))

    def banks(self, n=8):
        return [self.ctx.enter_context(self.nc.psum_tensor(f"{self.name}_bank{i}", [P, 512], F32)) for i in range(n)]

    def sem(self, name):
        if name.startswith("st_"):
            return self.nc.alloc_semaphore(f"{self.name}_{name}")
        s = self.ctx.enter_context(self.nc.semaphore(f"{self.name}_{name}"))
        self.nums.append(s.num)
        return s

    def block(self):
        return self.ctx.enter_context(self.nc.Block())


def three_pass(nc, out, w, x, k_tiles):
    for k in range(k_tiles):
        (wh, wl), (xh, xl) = w(k), x(k)
        nc.tensor.matmul(out, wh, xh, start=(k == 0), stop=False)
        nc.tensor.matmul(out, wh, xl, start=False, stop=False)
        last = nc.tensor.matmul(out, wl, xh, start=False, stop=(k == k_tiles - 1))
    return last


def phase_vectors(nc, d, g):
    NS = 3
    with Box(nc, "mod") as bx:
        w = bx.sb("w", [P, NS, KD, 512])
        cc = bx.sb("cc", [P, KD, 2])
        sil = bx.sb("sil", [P, KD, 2])
        silb = bx.sb("silb", [P, KD, P])
        bada = bx.sb("bada", [P, 48])
        lncol = bx.sb("lncol", [P, 4, KD])
        brow = bx.sb("brow", [P, 2, D])
        lgt = bx.sb("lgt", [P, 2, 2, H])
        m = bx.sb("m", [P, 2, H])
        e = bx.sb("e", [P, 2, 2, H])
        s = bx.sb("s", [P, 2, H])
        mc = bx.sb("mc", [P, 48, 2])
        bank = bx.banks()
        ld_small, ld_w = bx.sem("ld_small"), [bx.sem(f"ld_w{i}") for i in range(NS)]
        silu_done, dve_step, chunk_done, act_exp = bx.sem("silu_done"), bx.sem("dve_step"), bx.sem("chunk_done"), bx.sem("act_exp")
        silb_done = bx.sem("silb_done")
        NCH = 12
        block = bx.block()
        row_chunks = [4, 5, 10, 11]

        @block.sync
        def _(sp):
            for dst, src in ((cc[:], d["ccol"]), (bada[:], d["b_ada_col"]), (lncol[:], d["ln_cols"]),
                             (lgt[:], d["lb_logits"]),
                             (brow[:, 0, :], d["b_ada"][2 * D:3 * D].partition_broadcast(P)),
                             (brow[:, 1, :], d["b_ada"][5 * D:6 * D].partition_broadcast(P))):
                sp.dma_start(dst, src).then_inc(ld_small, 16)
            for j in range(NCH):
                if j >= NS:
                    sp.wait_ge(chunk_done, j - NS + 1)
                sp.dma_start(w[:, j % NS], d["w_ada"][:, j * 512:(j + 1) * 512].rearrange("(k p) n -> p k n", p=P)
                             ).then_inc(ld_w[j % NS], 16)

        @block.scalar
        def _(act):
            act.wait_ge(ld_small, 96)
            nc.scalar.activation(sil[:], cc[:], ACT.Silu).then_inc(silu_done, 1)
            act.wait_ge(dve_step, 3)
            nc.scalar.activation(e[:], e[:], ACT.Exp).then_inc(act_exp, 1)

        @block.tensor
        def _(pe):
            pe.wait_ge(silu_done, 1)
            pe.wait_ge(silb_done, 1)
            for j in range(NCH):
                pe.wait_ge(ld_w[j % NS], 16 * (j // NS + 1))
                if j in row_chunks:
                    out = bank[1 + row_chunks.index(j)]
                    for k in range(KD):
                        last = nc.tensor.matmul(out[:], silb[:, k, :], w[:, j % NS, k, :], start=(k == 0), stop=(k == KD - 1))
                else:
                    for mt in range(4):
                        col = (4 * j + mt) * 2
                        for k in range(KD):
                            last = nc.tensor.matmul(bank[0][:, col:col + 2], w[:, j % NS, k, mt * P:(mt + 1) * P],
                                                    sil[:, k, :], start=(k == 0), stop=(k == KD - 1))
                last.then_inc(chunk_done, 1)

        @block.vector
        def _(dve):
            step = Count(dve_step)
            dve.wait_ge(ld_small, 96)
            step.up(nc.vector.tensor_tensor(m[:], lgt[:, :, 0, :], lgt[:, :, 1, :], ALU.max))
            step.wait(dve)
            for i in range(2):
                step.up(nc.vector.tensor_tensor(e[:, :, i, :], lgt[:, :, i, :], m[:], ALU.subtract))
            dve.wait_ge(silu_done, 1)
            nc.vector.tensor_copy(silb[:], sil[:, :, 0:1].to_broadcast([P, KD, P])).then_inc(silb_done, 1)
            dve.wait_ge(act_exp, 1)
            step.up(nc.vector.tensor_tensor(s[:], e[:, :, 0, :], e[:, :, 1, :], ALU.add))
            step.wait(dve)
            step.up(nc.vector.reciprocal(m[:], s[:]))
            step.wait(dve)
            step.up(nc.vector.tensor_tensor(g["lb"][:], e[:, :, 0, :], m[:], ALU.mult))
            step.wait(dve)
            step.up(nc.vector.tensor_scalar(g["oml"][:], g["lb"][:], -1.0, 1.0, ALU.mult, ALU.add))
            dve.wait_ge(chunk_done, NCH)
            for a, b in ((0, 16), (24, 40)):
                step.up(nc.vector.tensor_tensor(mc[:, a:b, :], bank[0][:, 2 * a:2 * b].rearrange("p (a b) -> p a b", b=2),
                                                bada[:, a:b].rearrange("p (a b) -> p a b", b=1).to_broadcast([P, b - a, 2]), ALU.add))
            for r, name in enumerate(("mod2", "mod5")):
                for c in range(2):
                    step.up(nc.vector.tensor_tensor(g[name][:, c * 512:(c + 1) * 512], bank[1 + 2 * r + c][:],
                                                    brow[:, r, c * 512:(c + 1) * 512], ALU.add))
            step.wait(dve)
            for i, (who, sh, lng) in enumerate(((0, 0, 0), (1, 0, 0), (0, 3, 2))):
                sc, bi = g["scale"][:, i, :], g["shift"][:, i, :]
                one = mc[:, (sh + 1) * 8:(sh + 2) * 8, who]
                step.up(nc.vector.scalar_tensor_tensor(sc, one, 1.0, lncol[:, lng, :], ALU.add, ALU.mult))
                step.up(nc.vector.scalar_tensor_tensor(bi, one, 1.0, lncol[:, lng + 1, :], ALU.add, ALU.mult))
                step.wait(dve)
                step.up(nc.vector.tensor_tensor(bi, bi, mc[:, sh * 8:(sh + 1) * 8, who], ALU.add))


def phase_norm_transpose(nc, d, g, name, src, groups, tiles, which, out_hi, out_lo, pos=None, norm=True, xn_out=None):
    W = tiles * P
    with Box(nc, name) as bx:
        x = bx.sb("x", [P, 2 if norm else 1, tiles, D])
        xn = bx.sb("xn", [P, tiles, D]) if norm else None
        pr = bx.sb("pr", [P, tiles, BR]) if pos else None
        pc = bx.sb("pc", [P, 1, BR]) if pos else None
        hf = bx.sb("hf", [P, 2, W])
        stats = bx.sb("stats", [P, tiles, 2, 6])
        mv = bx.sb("mv", [P, tiles, 2])
        std = bx.sb("std", [P, tiles])
        rstd = bx.sb("rstd", [P, tiles])
        bank = bx.banks()
        ld_x, ld_c, st_x = bx.sem("ld_x"), bx.sem("ld_c"), bx.sem("st_x")
        x_free, std_done, xn_ready = bx.sem("x_free"), bx.sem("std_done"), bx.sem("xn_ready")
        xT, evac, split, step_s, mv_done = bx.sem("xT"), bx.sem("evac"), bx.sem("split"), bx.sem("step"), bx.sem("mv_done")
        block = bx.block()
        nld = 48 if pos else 16

        @block.sync
        def _(sp):
            if pos:
                sp.dma_start(pc[:, 0, :], pos[1]).then_inc(ld_c, 16)
            with repeat(sp, 0, groups, {}) as gi:
                sp.wait_ge(x_free, gi + 1)
                sp.dma_start(x[:, 0], src[bass.ds(gi * W, W), :].rearrange("(s p) n -> p s n", p=P)).then_inc(ld_x, 16)
                if pos:
                    er = pos[0].rearrange("(r h) n -> h r n", h=2)
                    for h in range(2):
                        sp.dma_start(pr[64 * h:64 * h + 64], er[h, bass.ds(gi * tiles, tiles), :].partition_broadcast(64)
                                     ).then_inc(ld_x, 16)

        if norm:
            @block.vector
            def _(dve):
                step = Count(step_s)
                dve.sem_inc(x_free, 1)
                if pos:
                    dve.wait_ge(ld_c, 16)
                with repeat(dve, 0, groups, {step: 4 * tiles - 1 + 2 * bool(pos) + KD}) as gi:
                    dve.wait_ge(ld_x, (gi + 1) * nld)
                    if pos:
                        step.up(nc.vector.tensor_tensor(x[:, 0, :, 0:BR], x[:, 0, :, 0:BR], pr[:], ALU.add))
                        step.up(nc.vector.tensor_tensor(x[:, 0, :, BR:D], x[:, 0, :, BR:D],
                                                        pc[:].to_broadcast([P, tiles, BR]), ALU.add))
                        step.wait(dve)
                    for s in range(tiles):
                        for c in range(2):
                            step.up(nc.vector.bn_stats(stats[:, s, c, :], x[:, 0, s, c * 512:(c + 1) * 512]))
                    step.wait(dve)
                    settle(dve, g)
                    for s in range(tiles):
                        last = nc.vector.bn_aggr(mv[:, s, :], stats[:, s].rearrange("p a b -> p (a b)"))
                        if s < tiles - 1:
                            step.up(last)
                    last.then_inc(mv_done, 1)
                    dve.wait_ge(std_done, gi + 1)
                    step.up(nc.vector.reciprocal(rstd[:], std[:]))
                    step.wait(dve)
                    if xn_out is not None:
                        dve.wait_ge(st_x, gi * 16 + 16)
                    dve.wait_ge(xT, gi * KD + KD)
                    dve.wait_ge(mv_done, gi + 1)
                    for s in range(tiles):
                        last = nc.vector.tensor_scalar(xn[:, s, :], x[:, 0, s, :], mv[:, s, 0:1], rstd[:, s:s + 1],
                                                       ALU.subtract, ALU.mult)
                        if s < tiles - 1:
                            step.up(last, 1)
                    last.then_inc(xn_ready, 1)
                    dve.wait_ge(xn_ready, gi + 1)
                    dve.sem_inc(x_free, 1)
                    for k in range(KD):
                        hi = out_hi[:, k, bass.ds(gi * W, W)]
                        dve.wait_ge(evac, gi * KD + KD + k + 1)
                        step.up(nc.vector.tensor_copy(hi, hf[:, k % 2, :]))
                        step.wait(dve)
                        nc.vector.tensor_tensor(out_lo[:, k, bass.ds(gi * W, W)], hf[:, k % 2, :], hi.bitcast(F32),
                                                ALU.subtract).then_inc(split, 1)
        else:
            @block.vector
            def _(dve):
                step = Count(step_s)
                with repeat(dve, 0, groups, {step: KD}) as gi:
                    for k in range(KD):
                        hi = out_hi[:, k, bass.ds(gi * W, W)]
                        dve.wait_ge(evac, gi * KD + KD + k + 1)
                        step.up(nc.vector.tensor_copy(hi, hf[:, k % 2, :]))
                        step.wait(dve)
                        nc.vector.tensor_tensor(out_lo[:, k, bass.ds(gi * W, W)], hf[:, k % 2, :], hi.bitcast(F32),
                                                ALU.subtract).then_inc(split, 1)

        @block.scalar
        def _(act):
            act.sem_inc(evac, KD)
            act.sem_inc(split, 2)
            with repeat(act, 0, groups, {}) as gi:
                if norm:
                    act.wait_ge(mv_done, gi + 1)
                    nc.scalar.activation(std[:], mv[:, :, 1], ACT.Sqrt, bias=g["eps"][:, 0:1]).then_inc(std_done, 1)
                for k in range(KD):
                    act.wait_ge(xT, gi * KD + k + 1 + KD)
                    act.wait_ge(split, gi * KD + k + 1)
                    nc.scalar.activation(hf[:, k % 2, :], bank[k][:, 0:W], ACT.Identity, bias=g["shift"][:, which, k:k + 1],
                                         scale=g["scale"][:, which, k:k + 1]).then_inc(evac, 1)

        @block.tensor
        def _(pe):
            pe.sem_inc(xT, KD)
            if not norm:
                pe.sem_inc(x_free, 1)
            with repeat(pe, 0, groups, {}) as gi:
                if norm:
                    pe.wait_ge(xn_ready, gi + 1)
                else:
                    pe.wait_ge(ld_x, (gi + 1) * nld)
                for k in range(KD):
                    pe.wait_ge(evac, gi * KD + k + 1)
                    for s in range(tiles):
                        from_ = xn[:, s, k * P:(k + 1) * P] if norm else x[:, 0, s, k * P:(k + 1) * P]
                        last = nc.tensor.transpose(bank[k][:, s * P:(s + 1) * P], from_, g["ident"][:])
                    last.then_inc(xT, 1)
                if not norm:
                    pe.wait_ge(xT, (gi + 1) * KD + KD)
                    pe.sem_inc(x_free, 1)

        @block.gpsimd
        def _(pool):
            if xn_out is not None:
                prime(pool, d, g, [st_x])
                with repeat(pool, 0, groups, {}) as gi:
                    pool.wait_ge(xn_ready, gi + 1)
                    pool.dma_start(xn_out[bass.ds(gi * W, W), :].rearrange("(s p) n -> p s n", p=P), xn[:]).then_inc(st_x, 16)
                pool.wait_ge(st_x, 16 * (groups + 1))


def phase_project(nc, d, g, hT, cT):
    secs = [(C_FF, 8, ACT.Sigmoid, "ctx", 0, True),
            (C_FF, 8, ACT.Sigmoid, "lat", R_F, True),
            (C_G, 16, ACT.Sigmoid, "lat", R_G, False),
            (C_Q, 4, ACT.Silu, "lat", R_Q, False),
            (C_OG, 4, ACT.Silu, "lat", R_OG, False)]
    with Box(nc, "proj") as bx:
        raw = bx.sb("raw", [P, 2, KD, P])
        wh = bx.sb("wh", [P, 2, KD, P], F32R)
        wl = bx.sb("wl", [P, 2, KD, P], F32R)
        stage = bx.sb("stage", [P, 2, T])
        bank = bx.banks()
        ld_w = [bx.sem(f"ld_w{i}") for i in range(2)]
        st_o = [bx.sem(f"st_o{i}") for i in range(2)]
        w_hi, w_split, strip_done, mm_done, evac, f_done = (bx.sem(n) for n in (
            "w_hi", "w_split", "strip_done", "mm_done", "evac", "f_done"))
        block = bx.block()
        lbv = g["lb"][:].rearrange("p a b -> p (a b)")
        omv = g["oml"][:].rearrange("p a b -> p (a b)")

        @block.sync
        def _(sp):
            n0 = 0
            for col, n, _, _, _, _ in secs:
                with sp.Fori(0, n // 2) as i:
                    for s in range(2):
                        sp.wait_ge(w_split, i * 2 + (n0 + s + 1))
                        sp.dma_start(raw[:, s], d["w_in"][:, bass.ds(i * 2 * P + (col + s * P), P)].rearrange("(k p) n -> p k n", p=P)
                                     ).then_inc(ld_w[s], 16)
                n0 += n

        @block.vector
        def _(dve):
            dve.sem_inc(w_split, 2)
            n0 = 0
            for _, n, _, _, _, _ in secs:
                with dve.Fori(0, n // 2) as i:
                    for s in range(2):
                        dve.wait_ge(ld_w[s], i * 16 + (n0 * 8 + 16))
                        dve.wait_ge(strip_done, i * 2 + (n0 + s + 1))
                        nc.vector.tensor_copy(wh[:, s], raw[:, s]).then_inc(w_hi, 1)
                        dve.wait_ge(w_hi, i * 2 + (n0 + s + 1))
                        nc.vector.tensor_tensor(wl[:, s], raw[:, s], wh[:, s].bitcast(F32), ALU.subtract).then_inc(w_split, 1)
                n0 += n

        @block.tensor
        def _(pe):
            pe.sem_inc(strip_done, 2)
            n0 = 0
            ev0 = 0
            for col, n, _, who, _, _ in secs:
                nch, W = (4, 512) if who == "lat" else (1, TC)
                hi, lo = hT if who == "lat" else cT
                if ev0 == 8:
                    pe.wait_ge(evac, ev0 + 8)
                with pe.Fori(0, n // 2) as i:
                    for s in range(2):
                        pe.wait_ge(w_split, i * 2 + (n0 + s + 3))
                        for c in range(nch):
                            pe.wait_ge(evac, i * 2 * nch + (ev0 + s * nch + c + 1 + (0 if nch == 4 else 6)))
                            out = bank[(4 * s + c)][:, 0:W]
                            last = three_pass(nc, out, lambda k: (wh[:, s, k, :], wl[:, s, k, :]),
                                              lambda k: (hi[:, k, c * W:(c + 1) * W], lo[:, k, c * W:(c + 1) * W]), KD)
                            last.then_inc(mm_done, 1)
                        pe.wait_ge(mm_done, i * 2 * nch + (ev0 + (s + 1) * nch))
                        pe.sem_inc(strip_done, 1)
                n0 += n
                ev0 += n * nch

        @block.scalar
        def _(act):
            act.sem_inc(evac, 8)
            n0 = 0
            ev0 = 0
            for col, n, func, who, row, _ in secs:
                nch, W = (4, 512) if who == "lat" else (1, TC)
                with act.Fori(0, n // 2) as i:
                    for s in range(2):
                        act.wait_ge(st_o[s], i * 16 + (n0 * 8 + 16))
                        for c in range(nch):
                            act.wait_ge(mm_done, i * 2 * nch + (ev0 + s * nch + c + 1))
                            settle(act, g)
                            nc.scalar.activation(stage[:, s, c * W:(c + 1) * W], bank[4 * s + c][:, 0:W], func,
                                                 bias=g["b_in_col"][:, bass.ds(i * 2 + (col // P + s), 1)]).then_inc(evac, 1)
                n0 += n
                ev0 += n * nch

        @block.gpsimd
        def _(pool):
            n0 = 0
            ev0 = 0
            fdone = 0
            prime(pool, d, g, st_o)
            for col, n, _, who, row, is_f in secs:
                nch, W = (4, 512) if who == "lat" else (1, TC)
                dst = d["proj"] if who == "lat" else d["proj_ctx"]
                if is_f:
                    for m in range(n):
                        part = stage[:, m % 2, 0:nch * W]
                        pool.wait_ge(evac, ev0 + (m + 1) * nch + 8)
                        nc.gpsimd.tensor_scalar(part, part, omv[:, m:m + 1], lbv[:, m:m + 1], ALU.mult, ALU.add).then_inc(f_done, 1)
                        fdone += 1
                        pool.wait_ge(f_done, fdone)
                        pool.dma_start(dst[row + m * P:row + (m + 1) * P, :], part).then_inc(st_o[m % 2], 16)
                else:
                    with pool.Fori(0, n // 2) as i:
                        for s in range(2):
                            pool.wait_ge(evac, i * 2 * nch + (ev0 + (s + 1) * nch + 8))
                            pool.dma_start(dst[bass.ds(i * 2 * P + (row + s * P), P), :], stage[:, s, 0:nch * W]).then_inc(st_o[s], 16)
                n0 += n
                ev0 += n * nch
            for s in range(2):
                pool.wait_ge(st_o[s], 16 + 8 * n0)


def phase_project_tokens(nc, d, g, hT, cT):
    with Box(nc, "tok") as bx:
        raw = bx.sb("raw", [P, 2, BR])
        wh = bx.sb("wh", [P, KD, BR], F32R)
        wl = bx.sb("wl", [P, KD, BR], F32R)
        stage = bx.sb("stage", [P, 4, BR])
        brow = bx.sb("brow", [P, 2, BR])
        bank = bx.banks()
        ld_b, ld_w = bx.sem("ld_b"), [bx.sem(f"ld_w{i}") for i in range(2)]
        st_o = [bx.sem(f"st_o{i}") for i in range(4)]
        w_hi, w_split, mm_done, evac = bx.sem("w_hi"), bx.sem("w_split"), bx.sem("mm_done"), bx.sem("evac")
        block = bx.block()
        jobs = [(0, hT, n2, NTT, d["u"][n2]) for n2 in range(NTT)]
        jobs += [(1, cT, t * P, 1, d["v_ctx"][t * P:(t + 1) * P, :]) for t in range(TC // P)]
        jobs += [(1, hT, t * P, 1, d["v"][t * P:(t + 1) * P, :]) for t in range(NTT)]
        first_v = NTT

        @block.sync
        def _(sp):
            for i, c in enumerate((C_U, C_V)):
                sp.dma_start(brow[:, i, :], d["b_in"][c:c + BR].partition_broadcast(P)).then_inc(ld_b, 16)
            for n in range(2 * KD):
                if n >= 2:
                    sp.wait_ge(w_split, n - 1)
                c, k = (C_U, C_V)[n // KD], n % KD
                sp.dma_start(raw[:, n % 2, :], d["w_in"][k * P:(k + 1) * P, c:c + BR]).then_inc(ld_w[n % 2], 16)

        @block.vector
        def _(dve):
            def split(sec):
                if sec:
                    dve.wait_ge(mm_done, first_v)
                for k in range(KD):
                    n = sec * KD + k
                    dve.wait_ge(ld_w[n % 2], 16 * (n // 2 + 1))
                    nc.vector.tensor_copy(wh[:, k, :], raw[:, n % 2, :]).then_inc(w_hi, 1)
                    dve.wait_ge(w_hi, n + 1)
                    nc.vector.tensor_tensor(wl[:, k, :], raw[:, n % 2, :], wh[:, k, :].bitcast(F32), ALU.subtract).then_inc(w_split, 1)
            split(0)
            dve.wait_ge(ld_b, 32)
            for n, (sec, _, _, _, _) in enumerate(jobs):
                if n == first_v:
                    split(1)
                dve.wait_ge(mm_done, n + 1)
                if n >= 4:
                    dve.wait_ge(st_o[n % 4], 16 * (n // 4))
                nc.vector.tensor_tensor(stage[:, n % 4, :], bank[n % 8][:], brow[:, sec, :], ALU.add).then_inc(evac, 1)

        @block.tensor
        def _(pe):
            for n, (sec, (hi, lo), t0, st, _) in enumerate(jobs):
                if n in (0, first_v):
                    pe.wait_ge(w_split, KD * (sec + 1))
                if n >= 8:
                    pe.wait_ge(evac, n - 7)
                sl = slice(t0, t0 + st * (P - 1) + 1, st)
                three_pass(nc, bank[n % 8][:], lambda k: (hi[:, k, sl], lo[:, k, sl]),
                           lambda k: (wh[:, k, :], wl[:, k, :]), KD).then_inc(mm_done, 1)

        @block.gpsimd
        def _(pool):
            for n, job in enumerate(jobs):
                pool.wait_ge(evac, n + 1)
                pool.dma_start(job[4], stage[:, n % 4, :]).then_inc(st_o[n % 4], 16)
            for s in range(4):
                pool.wait_ge(st_o[s], 16 * len(range(s, len(jobs), 4)))


def phase_fourier(nc, d, g):
    N2 = NTT
    with Box(nc, "dft") as bx:
        m1 = bx.sb("m1", [P, N2, 2, P])
        m2 = bx.sb("m2", [P, 2, 2 * P])
        m3 = bx.sb("m3", [P, 2, P])
        u = bx.sb("u", [P, 4, BR])
        a_st = bx.sb("a_st", [P, 2, 2, BR])
        xin = bx.sb("xin", [P, 2, 2, BR])
        zT = bx.sb("zT", [P, H, 2, T])
        fst = bx.sb("fst", [P, 2, 512])
        bank = bx.banks()
        ld_m, ld_u, ld_x = bx.sem("ld_m"), [bx.sem(f"ld_u{i}") for i in range(4)], [bx.sem(f"ld_x{i}") for i in range(2)]
        st_a, st_f = [bx.sem(f"st_a{i}") for i in range(2)], [bx.sem(f"st_f{i}") for i in range(2)]
        mm1, ev1, mm2, ev2, mm3, ev3 = (bx.sem(n) for n in ("mm1", "ev1", "mm2", "ev2", "mm3", "ev3"))
        block = bx.block()
        a_d = d["dft_a"]

        @block.sync
        def _(sp):
            sp.dma_start(m1[:], d["dft_m1"]).then_inc(ld_m, 16)
            sp.dma_start(m2[:], d["dft_m2"]).then_inc(ld_m, 16)
            sp.dma_start(m3[:], d["dft_m3"]).then_inc(ld_m, 16)
            for n in range(N2):
                if n >= 4:
                    sp.wait_ge(mm1, n - 3)
                sp.dma_start(u[:, n % 4, :], d["u"][n]).then_inc(ld_u[n % 4], 16)
            for s in range(2):
                sp.wait_ge(st_a[s], 16 * N2 // 2)
            av = a_d.rearrange("n r (a b) c -> a r n b c", b=8)
            for a in range(N2):
                if a >= 2:
                    sp.wait_ge(mm2, 4 * (a - 1))
                for r in range(2):
                    for n in range(N2):
                        sp.dma_start(xin[8 * n:8 * n + 8, a % 2, r, :], av[a, r, n]).then_inc(ld_x[a % 2], 16)

        @block.tensor
        def _(pe):
            pe.wait_ge(ld_m, 48)
            for n in range(N2):
                pe.wait_ge(ld_u[n % 4], 16 * (n // 4 + 1))
                if n >= 4:
                    pe.wait_ge(ev1, n - 3)
                for r in range(2):
                    last = nc.tensor.matmul(bank[2 * (n % 4) + r][:], m1[:, n, r, :], u[:, n % 4, :], start=True, stop=True)
                last.then_inc(mm1, 1)
            pe.wait_ge(ev1, N2)
            for a in range(N2):
                pe.wait_ge(ld_x[a % 2], 16 * 2 * N2 * (a // 2 + 1))
                for h in range(H):
                    n = a * H + h
                    if n >= 8:
                        pe.wait_ge(ev2, n - 7)
                    for r in range(2):
                        last = nc.tensor.matmul(bank[n % 8][:, 0:2 * P], xin[:, a % 2, r, h * P:(h + 1) * P], m2[:, r, :],
                                                start=(r == 0), stop=(r == 1))
                    last.then_inc(mm2, 1)
            pe.wait_ge(ev2, N2 * H)
            for n in range(4 * H):
                h, c = n // 4, n % 4
                if n >= 8:
                    pe.wait_ge(ev3, n - 7)
                for r in range(2):
                    last = nc.tensor.matmul(bank[n % 8][:], m3[:, r, :], zT[:, h, r, c * 512:(c + 1) * 512],
                                            start=(r == 0), stop=(r == 1))
                last.then_inc(mm3, 1)

        @block.scalar
        def _(act):
            for n in range(N2):
                act.wait_ge(mm1, n + 1)
                if n >= 2:
                    act.wait_ge(st_a[n % 2], 16 * (n // 2))
                for r in range(2):
                    last = nc.scalar.copy(a_st[:, n % 2, r, :], bank[2 * (n % 4) + r][:])
                last.then_inc(ev1, 1)
            for n in range(4 * H):
                act.wait_ge(mm3, n + 1)
                if n >= 2:
                    act.wait_ge(st_f[n % 2], 16 * (n // 2))
                nc.scalar.copy(fst[:, n % 2, :], bank[n % 8][:]).then_inc(ev3, 1)

        @block.vector
        def _(dve):
            for n in range(N2 * H):
                a, h = n // H, n % H
                dve.wait_ge(mm2, n + 1)
                dst = zT[:, h].rearrange("p r (t2 a b) -> p (r t2) a b", a=N2, b=8)[:, :, a, :]
                nc.vector.tensor_copy(dst, bank[n % 8][:, 0:2 * P].rearrange("p (m b) -> p m b", b=8)).then_inc(ev2, 1)

        @block.gpsimd
        def _(pool):
            for n in range(N2):
                pool.wait_ge(ev1, n + 1)
                pool.dma_start(a_d[n].rearrange("r p c -> p r c"), a_st[:, n % 2]).then_inc(st_a[n % 2], 16)
            for n in range(4 * H):
                h, c = n // 4, n % 4
                pool.wait_ge(ev3, n + 1)
                pool.dma_start(d["four"][h * P:(h + 1) * P, c * 512:(c + 1) * 512], fst[:, n % 2, :]).then_inc(st_f[n % 2], 16)
            for s in range(2):
                pool.wait_ge(st_f[s], 16 * 2 * H)


def phase_hgrn(nc, d, g):
    with Box(nc, "hgrn") as bx:
        f = bx.sb("f", [P, 2, 2, H * P])
        q = bx.sb("q", [P, 2, 2, H * P])
        v = bx.sb("v", [P, 2, 2, BR])
        kk = bx.sb("kk", [P, 2, 2, H * P])
        suf = bx.sb("suf", [P, 2, H * P])
        lev = bx.sb("lev", [P, 2, NL, H * P])
        qd = bx.sb("qd", [P, 2, 2, H * P])
        kd = bx.sb("kd", [P, 2, 2, H * P])
        tot = bx.sb("tot", [P, 2, 2, H])
        pm = bx.sb("pm", [P, 2, H * P])
        kdT = bx.sb("kdT", [P, H * P])
        st = bx.sb("st", [P, 2, H * P])
        ost = bx.sb("ost", [P, 2, H * P])
        mask = bx.sb("mask", [P, 2, NL, 256], I32)
        diag = bx.sb("diag", [P, H * P], I32)
        bank = bx.banks()
        SC, DG, TR, OO, SS = bank[0:4], bank[4], bank[5], bank[6], bank[7]
        ld_m = bx.sem("ld_m")
        ld = [[bx.sem(f"ld_{x}{s}") for s in range(2)] for x in "fb"]
        step_s, st_o = bx.sem("step"), [bx.sem(f"st_o{x}") for x in "fb"]
        ready, scores, masked, trans, trcopy, o_mm, o_out, s_mm, s_new, init = (bx.sem(n) for n in (
            "lev_ready", "scores", "masked", "trans", "trcopy", "o_mm", "o_out", "s_mm", "s_new", "init"))
        block = bx.block()
        NC_, NX = NTT, TC // P
        RDY = NL + 1
        NXU = 2 * NX

        def cols(dr, j, n):
            return (j * P) if dr == 0 else ((n - 1) * P - j * P)

        def halves(ap, B):
            return ap.rearrange("p (m two b) -> p m two b", two=2, b=B)

        @block.sync
        def _(sp):
            sp.dma_start(mask[:], d["masks"]).then_inc(ld_m, 16)
            sp.dma_start(diag[:], d["diag"]).then_inc(ld_m, 16)
            for j in range(NX):
                for dr in range(2):
                    c = cols(dr, j, NX)
                    sp.dma_start(f[:, dr, j % 2], d["proj_ctx"][dr * BR:(dr + 1) * BR, c:c + P].rearrange("(h p) t -> p h t", p=P)
                                 ).then_inc(ld[dr][j % 2], 16)
                    sp.dma_start(v[:, dr, j % 2, :], d["v_ctx"][c:c + P, :]).then_inc(ld[dr][j % 2], 16)
            with sp.Fori(0, NC_ // 2) as i:
                for s in range(2):
                    for dr in range(2):
                        sp.wait_ge(s_mm, i * 4 + (NXU + 2 * s + dr + 1 - 4))
                        base = (P * s) if dr == 0 else ((NC_ - 1 - s) * P)
                        c = i * (2 * P if dr == 0 else -2 * P) + base
                        pf = d["proj"][R_F + dr * BR:R_F + (dr + 1) * BR, :]
                        pq = d["proj"][R_Q:R_Q + BR, :]
                        sp.dma_start(f[:, dr, s], pf[:, bass.ds(c, P)].rearrange("(h p) t -> p h t", p=P)).then_inc(ld[dr][s], 16)
                        sp.dma_start(q[:, dr, s], pq[:, bass.ds(c, P)].rearrange("(h p) t -> p h t", p=P)).then_inc(ld[dr][s], 16)
                        sp.dma_start(v[:, dr, s, :], d["v"][bass.ds(c, P), :]).then_inc(ld[dr][s], 16)

        @block.vector
        def _(dve):
            step, rdy, msk, snew = Count(step_s), Count(ready), Count(masked), Count(s_new)
            mm_ss, mm_sc = Count(s_mm), Count(scores)

            def gates(dr, s, latent):
                qh, kh = (1, 0) if dr == 0 else (0, 1)
                fu, qu, ku, su = f[:, dr, s], q[:, dr, s], kk[:, dr, s], suf[:, dr]
                step.up(nc.vector.tensor_scalar(ku, fu, -1.0, 1.0, ALU.mult, ALU.add))
                step.wait(dve)
                for li, B in enumerate(LEVELS):
                    fv, qv, kv, sv = halves(fu, B), halves(qu, B), halves(ku, B), halves(su, B)
                    lv = halves(lev[:, dr, li], B)
                    e = B - 1 if dr == 0 else 0
                    if latent:
                        step.up(nc.vector.tensor_tensor(lv[:, :, qh], qv[:, :, qh], fv[:, :, qh], ALU.mult))
                        if B == 1:
                            rdy.up(nc.vector.tensor_copy(lv[:, :, kh], kv[:, :, kh]))
                        else:
                            rdy.up(nc.vector.tensor_tensor(lv[:, :, kh], kv[:, :, kh], sv[:, :, kh], ALU.mult))
                    if B == 1:
                        step.up(nc.vector.memset(sv[:, :, qh], 1.0))
                        step.up(nc.vector.tensor_copy(sv[:, :, kh], fv[:, :, qh]))
                    else:
                        step.up(nc.vector.tensor_tensor(sv[:, :, kh], sv[:, :, kh],
                                                        fv[:, :, qh, e:e + 1].to_broadcast([P, 256 // B, B]), ALU.mult))
                    step.wait(dve)
                    step.up(nc.vector.tensor_tensor(fv[:, :, qh], fv[:, :, qh],
                                                    fv[:, :, kh, e:e + 1].to_broadcast([P, 256 // B, B]), ALU.mult))
                    step.wait(dve)
                e = P - 1 if dr == 0 else 0
                if latent:
                    step.up(nc.vector.tensor_tensor(qd[:, dr, s], qu, fu, ALU.mult))
                step.up(nc.vector.tensor_copy(tot[:, dr, s], fu.rearrange("p (h t) -> p h t", h=H)[:, :, e]))
                rdy.up(nc.vector.tensor_tensor(kd[:, dr, s], ku, su, ALU.mult))

            def mask_scores(dr):
                qh = 1 - dr
                for li, B in enumerate(LEVELS):
                    if li % 2 == 0:
                        mm_sc.n += 1
                        mm_sc.wait(dve)
                    if li:
                        msk.wait(dve)
                    settle(dve, g)
                    msk.up(nc.vector.copy_predicated(halves(pm[:, dr], B)[:, :, qh],
                                                     mask[:, dr, li].rearrange("p (m b) -> p m b", b=B),
                                                     SC[li // 2][:, (li % 2) * 256:(li % 2) * 256 + 256].rearrange("p (m b) -> p m b", b=B)))
                mm_sc.n += 1
                mm_sc.wait(dve)
                msk.wait(dve)
                settle(dve, g)
                msk.up(nc.vector.copy_predicated(pm[:, dr], diag[:], DG[:]))

            def new_state(dr, s):
                mm_ss.n += 1
                mm_ss.wait(dve)
                for h in range(H):
                    c = slice(h * P, (h + 1) * P)
                    last = nc.vector.scalar_tensor_tensor(st[:, dr, c], st[:, dr, c], tot[:, dr, s, h:h + 1], SS[:, c],
                                                          ALU.mult, ALU.add)
                    if h < H - 1:
                        step.up(last)
                snew.up(last)

            step.up(nc.vector.memset(st[:], 0.0))
            step.up(nc.vector.memset(pm[:], 0.0))
            for j in range(NX):
                for dr in range(2):
                    dve.wait_ge(ld[dr][j % 2], 32 * (j // 2 + 1))
                    gates(dr, j % 2, False)
                    new_state(dr, j % 2)
            dve.wait_ge(ld_m, 32)
            g_step = 1 + NL * 3 + 1 + 2
            per = {step: 4 * (g_step + H - 1), rdy: 4 * RDY, msk: 4 * (NL + 1), snew: 4, mm_ss: 4, mm_sc: 4 * 5}
            with repeat(dve, 0, NC_ // 2, per) as i:
                for s in range(2):
                    for dr in range(2):
                        dve.wait_ge(ld[dr][s], i * 48 + (32 * (NX // 2) + 48))
                        gates(dr, s, True)
                    for dr in range(2):
                        mask_scores(dr)
                        new_state(dr, s)

        @block.tensor
        def _(pe):
            rdy, trc, sn, msk = Count(ready), Count(trcopy), Count(s_new), Count(masked)
            oo, sc, tr, omm, smm = Count(o_out), Count(scores), Count(trans), Count(o_mm), Count(s_mm)

            def transpose_keys(dr, s):
                rdy.n += 1
                rdy.wait(pe)
                for h in range(H):
                    last = nc.tensor.transpose(TR[:, h * P:(h + 1) * P], kd[:, dr, s, h * P:(h + 1) * P], g["ident"][:])
                tr.up(last)

            def state_product(dr, s):
                trc.n += 1
                trc.wait(pe)
                for h in range(H):
                    c = slice(h * P, (h + 1) * P)
                    last = nc.tensor.matmul(SS[:, c], kdT[:, c], v[:, dr, s, c], start=True, stop=True)
                smm.up(last)

            first = True
            for j in range(NX):
                for dr in range(2):
                    transpose_keys(dr, j % 2)
                    if not first:
                        sn.n += 1
                        sn.wait(pe)
                    first = False
                    state_product(dr, j % 2)
            per = {rdy: 4 * RDY, trc: 4, sn: 4, msk: 4 * (NL + 1), oo: 4, sc: 20, tr: 4, omm: 4, smm: 4}
            oo.n = 1
            with repeat(pe, 0, NC_ // 2, per) as i:
                for s in range(2):
                    for dr in range(2):
                        qh = 1 - dr
                        sn.n += 1
                        sn.wait(pe)
                        for li, B in enumerate(LEVELS):
                            rdy.n += 1
                            rdy.wait(pe)
                            for h in range(H):
                                lv = lev[:, dr, li, h * P:(h + 1) * P]
                                last = nc.tensor.matmul(SC[li // 2][:, (li % 2) * 256 + h * 64:(li % 2) * 256 + h * 64 + 64],
                                                        lv, halves(lv, B)[:, :, qh], start=True, stop=True)
                            if li % 2 == 1 or li == NL - 1:
                                sc.up(last)
                        for h in range(H):
                            c = slice(h * P, (h + 1) * P)
                            last = nc.tensor.matmul(DG[:, c], kk[:, dr, s, c], q[:, dr, s, c], start=True, stop=True)
                        sc.up(last)
                        transpose_keys(dr, s)
                        msk.n += NL + 1
                        msk.wait(pe)
                        oo.wait(pe)
                        oo.n += 1
                        for h in range(H):
                            c = slice(h * P, (h + 1) * P)
                            nc.tensor.matmul(OO[:, c], v[:, dr, s, c], pm[:, dr, c], start=True, stop=False)
                            last = nc.tensor.matmul(OO[:, c], st[:, dr, c], qd[:, dr, s, c], start=False, stop=True)
                        omm.up(last)
                        state_product(dr, s)

        @block.scalar
        def _(act):
            tr, smm, omm = Count(trans), Count(s_mm), Count(o_mm)
            trc, oo = Count(trcopy), Count(o_out, 1)
            act.sem_inc(o_out, 1)

            def copy_keys():
                tr.n += 1
                tr.wait(act)
                trc.up(nc.scalar.copy(kdT[:], TR[:]))
            for n in range(NXU):
                if n:
                    smm.n += 1
                    smm.wait(act)
                copy_keys()
            with repeat(act, 0, NC_ // 2, {tr: 4, smm: 4, omm: 4, trc: 4, oo: 4}) as i:
                for s in range(2):
                    for dr in range(2):
                        smm.n += 1
                        smm.wait(act)
                        copy_keys()
                        omm.n += 1
                        omm.wait(act)
                        act.wait_ge(st_o[dr], i * 32 + (16 * s + 16))
                        oo.up(nc.scalar.copy(ost[:, dr], OO[:]))

        @block.gpsimd
        def _(pool):
            oo = Count(o_out, 1)
            prime(pool, d, g, st_o)
            with repeat(pool, 0, NC_ // 2, {oo: 4}) as i:
                for s in range(2):
                    for dr in range(2):
                        oo.n += 1
                        oo.wait(pool)
                        base = (P * s) if dr == 0 else ((NC_ - 1 - s) * P)
                        c = i * (2 * P if dr == 0 else -2 * P) + base
                        pool.dma_start(d["o"][dr][:, bass.ds(c, P)].rearrange("(h p) t -> p h t", p=P),
                                       ost[:, dr].rearrange("p (h t) -> p h t", h=H)).then_inc(st_o[dr], 16)
            for dr in range(2):
                pool.wait_ge(st_o[dr], 16 + 16 * NC_)


def split_weights(nc, dve, raw, wh, wl, n, slices, ld_w, hi_s, lo_s, width):
    for k in range(slices):
        m = n + k
        dve.wait_ge(ld_w[m % 2], 16 * (m // 2 + 1))
        nc.vector.tensor_copy(wh[:, k, :], raw[:, m % 2, 0:width]).then_inc(hi_s, 1)
        dve.wait_ge(hi_s, m + 1)
        nc.vector.tensor_tensor(wl[:, k, :], raw[:, m % 2, 0:width], wh[:, k, :].bitcast(F32), ALU.subtract).then_inc(lo_s, 1)


def phase_merge(nc, d, g):
    with Box(nc, "merge") as bx:
        raw = bx.sb("raw", [P, 2, D])
        wfh, wfl = bx.sb("wfh", [P, KB, D], F32R), bx.sb("wfl", [P, KB, D], F32R)
        wph, wpl = bx.sb("wph", [P, KB, D], F32R), bx.sb("wpl", [P, KB, D], F32R)
        four = bx.sb("four", [P, KB, 512])
        o2 = bx.sb("o2", [P, 2, KB, 512])
        og = bx.sb("og", [P, KB, 512])
        sq = bx.sb("sq", [P, KB, 512])
        rms = bx.sb("rms", [P, KB, 512])
        fh, fl = bx.sb("fh", [P, KB, 512], F32R), bx.sb("fl", [P, KB, 512], F32R)
        oh, ol = bx.sb("oh", [P, KB, 512], F32R), bx.sb("ol", [P, KB, 512], F32R)
        gates = bx.sb("gates", [P, 2, 2, 512])
        t1 = bx.sb("t1", [P, 2, 512])
        y = bx.sb("y", [P, 2, 512])
        ng = bx.sb("ng", [P, KB])
        bank = bx.banks()
        ld_n, ld_w, ld_b = bx.sem("ld_n"), [bx.sem(f"ld_w{i}") for i in range(2)], bx.sem("ld_b")
        ld_g, st_y = [bx.sem(f"ld_g{i}") for i in range(2)], [bx.sem(f"st_y{i}") for i in range(2)]
        hi_s, lo_s, step_s, sum_s, sq_s, ms_s, rt_s, in_s, mm_s, y_s, used = (bx.sem(n) for n in (
            "w_hi", "w_lo", "step", "o_sum", "o_sq", "ms_mm", "rms", "operands", "mm", "y_done", "block_free"))
        block = bx.block()
        NB = T // 512

        @block.sync
        def _(sp):
            sp.dma_start(ng[:], d["norm_g_col"]).then_inc(ld_n, 16)
            for n in range(2 * KB):
                if n >= 2:
                    sp.wait_ge(lo_s, n - 1)
                w = (d["w_four"], d["w_hgrn"])[n // KB]
                sp.dma_start(raw[:, n % 2, :], w[(n % KB) * P:(n % KB + 1) * P, :]).then_inc(ld_w[n % 2], 16)
            with sp.Fori(0, NB) as b:
                sp.wait_ge(used, b + 1)
                tk = bass.ds(b * 512, 512)
                for dst, src in ((four[:], d["four"]), (o2[:, 0], d["o"][0]), (o2[:, 1], d["o"][1]),
                                 (og[:], d["proj"][R_OG:R_OG + BR, :])):
                    sp.dma_start(dst, src[:, tk].rearrange("(h p) t -> p h t", p=P)).then_inc(ld_b, 16)
                for m in range(KD):
                    sp.wait_ge(y_s, b * KD + (m + 1))
                    src = d["proj"][R_G:R_G + 2 * D, :].rearrange("(g m p) t -> m p g t", g=2, p=P)
                    sp.dma_start(gates[:, m % 2], src[m][:, :, tk]).then_inc(ld_g[m % 2], 16)

        @block.vector
        def _(dve):
            dve.sem_inc(used, 1)
            dve.sem_inc(y_s, 2)
            step, yc, sums = Count(step_s), Count(y_s, 2), Count(sum_s)
            split_weights(nc, dve, raw, wfh, wfl, 0, KB, ld_w, hi_s, lo_s, D)
            split_weights(nc, dve, raw, wph, wpl, KB, KB, ld_w, hi_s, lo_s, D)
            dve.wait_ge(ld_n, 16)
            ins = Count(in_s)
            with repeat(dve, 0, NB, {step: 1 + KB + 1 + 1 + 2 * KD, yc: KD, sums: 1, ins: 2}) as b:
                dve.wait_ge(ld_b, b * 64 + 64)
                sums.up(nc.vector.tensor_tensor(o2[:, 0], o2[:, 0], o2[:, 1], ALU.add))
                dve.wait_ge(mm_s, b * KD + KD)
                step.up(nc.vector.tensor_copy(fh[:], four[:]))
                step.wait(dve)
                ins.up(nc.vector.tensor_tensor(fl[:], four[:], fh[:].bitcast(F32), ALU.subtract))
                sums.wait(dve)
                dve.wait_ge(rt_s, b + 1)
                step.up(nc.vector.reciprocal(rms[:], rms[:]))
                step.wait(dve)
                for h in range(KB):
                    step.up(nc.vector.scalar_tensor_tensor(sq[:, h], o2[:, 0, h], ng[:, h:h + 1], rms[:, h], ALU.mult, ALU.mult))
                step.wait(dve)
                step.up(nc.vector.tensor_tensor(sq[:], sq[:], og[:], ALU.mult))
                step.wait(dve)
                nc.vector.tensor_copy(oh[:], sq[:]).then_inc(used, 1)
                dve.wait_ge(used, b + 2)
                ins.up(nc.vector.tensor_tensor(ol[:], sq[:], oh[:].bitcast(F32), ALU.subtract))
                for m in range(KD):
                    dve.wait_ge(ld_g[m % 2], b * (16 * KD // 2) + 16 * (m // 2 + 1))
                    dve.wait_ge(mm_s, b * KD + (KD + m + 1))
                    dve.wait_ge(st_y[m % 2], b * (16 * KD // 2) + 16 * (m // 2 + 1))
                    pb = bank[2 * (m % 4):2 * (m % 4) + 2]
                    step.up(nc.vector.tensor_tensor(t1[:, m % 2, :], gates[:, m % 2, 0, :], pb[0][:], ALU.mult))
                    step.up(nc.vector.tensor_tensor(y[:, m % 2, :], gates[:, m % 2, 1, :], pb[1][:], ALU.mult))
                    step.wait(dve)
                    yc.up(nc.vector.tensor_tensor(y[:, m % 2, :], y[:, m % 2, :], t1[:, m % 2, :], ALU.add))

        @block.scalar
        def _(act):
            with act.Fori(0, NB) as b:
                act.wait_ge(sum_s, b + 1)
                act.wait_ge(used, b + 1)
                nc.scalar.activation(sq[:], o2[:, 0], ACT.Square).then_inc(sq_s, 1)
                act.wait_ge(ms_s, b + 2)
                for h in range(KB):
                    last = nc.scalar.activation(rms[:, h], bank[h][:], ACT.Sqrt, bias=g["eps"][:, 1:2])
                last.then_inc(rt_s, 1)

        @block.tensor
        def _(pe):
            pe.sem_inc(mm_s, KD)
            pe.sem_inc(ms_s, 1)
            pe.wait_ge(lo_s, 2 * KB)
            with pe.Fori(0, NB) as b:
                pe.wait_ge(sq_s, b + 1)
                pe.wait_ge(y_s, b * KD + 2)
                for h in range(KB):
                    last = nc.tensor.matmul(bank[h][:], g["mean"][:], sq[:, h], start=True, stop=True)
                last.then_inc(ms_s, 1)
                pe.wait_ge(in_s, b * 2 + 2)
                for m in range(KD):
                    if m >= 4:
                        pe.wait_ge(y_s, b * KD + (m - 4 + 1 + 2))
                    c = slice(m * P, (m + 1) * P)
                    pb = bank[2 * (m % 4):2 * (m % 4) + 2]
                    three_pass(nc, pb[0][:], lambda k: (wfh[:, k, c], wfl[:, k, c]), lambda k: (fh[:, k], fl[:, k]), KB)
                    three_pass(nc, pb[1][:], lambda k: (wph[:, k, c], wpl[:, k, c]), lambda k: (oh[:, k], ol[:, k]), KB
                               ).then_inc(mm_s, 1)

        @block.gpsimd
        def _(pool):
            prime(pool, d, g, st_y)
            with pool.Fori(0, NB) as b:
                for m in range(KD):
                    pool.wait_ge(y_s, b * KD + (m + 3))
                    pool.dma_start(d["y"][m * P:(m + 1) * P, bass.ds(b * 512, 512)], y[:, m % 2, :]).then_inc(st_y[m % 2], 16)
            for s in range(2):
                pool.wait_ge(st_y[s], 16 + 16 * NB * KD // 2)


def layernorm_rows(nc, g, dve, step, r, stats, mv, mv_done, std_wait, std, rstd, out, sig):
    for c in range(2):
        step.up(nc.vector.bn_stats(stats[:, c, :], r[:, c * 512:(c + 1) * 512]))
    step.wait(dve)
    settle(dve, g)
    mv_done.up(nc.vector.bn_aggr(mv, stats.rearrange("p a b -> p (a b)")))
    mv_done.wait(dve)
    std_wait()
    step.up(nc.vector.reciprocal(rstd, std))
    step.wait(dve)
    sig.up(nc.vector.tensor_scalar(out, r, mv[:, 0:1], rstd, ALU.subtract, ALU.mult))


def phase_out_proj(nc, d, g):
    with Box(nc, "outp") as bx:
        raw = bx.sb("raw", [P, 2, D])
        wh, wl = bx.sb("wh", [P, KD, D], F32R), bx.sb("wl", [P, KD, D], F32R)
        y = bx.sb("y", [P, KD, 512])
        yh, yl = bx.sb("yh", [P, KD, 512], F32R), bx.sb("yl", [P, KD, 512], F32R)
        xn = bx.sb("xn", [P, 2, D])
        r = bx.sb("r", [P, 2, D])
        xo = bx.sb("xo", [P, 2, D])
        ag, rb, tmp = bx.sb("ag", [P, D]), bx.sb("rb", [P, D]), bx.sb("tmp", [P, D])
        stats, mv, std, rstd = bx.sb("stats", [P, 2, 6]), bx.sb("mv", [P, 2]), bx.sb("std", [P, 1]), bx.sb("rstd", [P, 1])
        bank = bx.banks()
        ld_v, ld_w, ld_y = bx.sem("ld_v"), [bx.sem(f"ld_w{i}") for i in range(2)], bx.sem("ld_y")
        ld_x, st_x = [bx.sem(f"ld_x{i}") for i in range(2)], [bx.sem(f"st_x{i}") for i in range(2)]
        hi_s, lo_s, step_s, yh_s, yl_s, mm_s, rd_s, mv_s, std_s, xo_s, xr_s, blk_s = (bx.sem(n) for n in (
            "w_hi", "w_lo", "step", "y_hi", "y_lo", "mm", "psum_read", "mv_done", "std", "xn1", "xn_read", "blk"))
        block = bx.block()
        NB = T // 512

        @block.sync
        def _(sp):
            for dst, src in ((ag, "ln_in_g"), (rb, "ln_in_b"), (tmp, "b_out")):
                sp.dma_start(dst[:], d[src].partition_broadcast(P)).then_inc(ld_v, 16)
            for n in range(KD):
                if n >= 2:
                    sp.wait_ge(lo_s, n - 1)
                sp.dma_start(raw[:, n % 2, :], d["w_out"][n * P:(n + 1) * P, :]).then_inc(ld_w[n % 2], 16)
            with sp.Fori(0, NB) as b:
                sp.wait_ge(yl_s, b + 1)
                sp.dma_start(y[:], d["y"][:, bass.ds(b * 512, 512)].rearrange("(k p) t -> p k t", p=P)).then_inc(ld_y, 16)
                for t in range(4):
                    sp.wait_ge(xr_s, b * 4 + (t + 1))
                    sp.dma_start(xn[:, t % 2, :], d["xn"][bass.ds(b * 512 + t * P, P), :]).then_inc(ld_x[t % 2], 16)

        @block.vector
        def _(dve):
            step, rd, xr, mvd, xo_c = Count(step_s), Count(rd_s, 4), Count(xr_s, 2), Count(mv_s), Count(xo_s)
            dve.sem_inc(yl_s, 1)
            dve.sem_inc(rd_s, 4)
            dve.sem_inc(xr_s, 2)
            dve.wait_ge(ld_v, 48)
            step.up(nc.vector.tensor_tensor(tmp[:], tmp[:], g["mod2"][:], ALU.mult))
            step.up(nc.vector.tensor_scalar(ag[:], ag[:], ALPHA, None, ALU.mult))
            step.wait(dve)
            step.up(nc.vector.scalar_tensor_tensor(rb[:], rb[:], ALPHA, tmp[:], ALU.mult, ALU.add))
            step.wait(dve)
            split_weights(nc, dve, raw, wh, wl, 0, KD, ld_w, hi_s, lo_s, D)
            with repeat(dve, 0, NB, {step: 4 * 5, rd: 8, xr: 4, mvd: 4, xo_c: 4}) as b:
                dve.wait_ge(ld_y, b * 16 + 16)
                dve.wait_ge(mm_s, b * 8 + 8)
                nc.vector.tensor_copy(yh[:], y[:]).then_inc(yh_s, 1)
                dve.wait_ge(yh_s, b + 1)
                nc.vector.tensor_tensor(yl[:], y[:], yh[:].bitcast(F32), ALU.subtract).then_inc(yl_s, 1)
                for t in range(4):
                    s = t % 2
                    dve.wait_ge(ld_x[s], b * 32 + 16 * (t // 2 + 1))
                    step.up(nc.vector.tensor_tensor(xn[:, s, :], xn[:, s, :], ag[:], ALU.mult))
                    step.wait(dve)
                    step.up(nc.vector.tensor_tensor(xn[:, s, :], xn[:, s, :], rb[:], ALU.add))
                    for c in range(2):
                        cs = slice(c * 512, (c + 1) * 512)
                        dve.wait_ge(mm_s, b * 8 + (8 + 2 * t + c + 1))
                        rd.up(nc.vector.tensor_tensor(r[:, s, cs], bank[2 * s + c][:], g["mod2"][:, cs], ALU.mult))
                    step.wait(dve)
                    rd.wait(dve)
                    xr.up(nc.vector.tensor_tensor(r[:, s, :], r[:, s, :], xn[:, s, :], ALU.add))
                    xr.wait(dve)
                    dve.wait_ge(st_x[s], b * 32 + 16 * (t // 2 + 1))
                    layernorm_rows(nc, g, dve, step, r[:, s, :], stats[:], mv[:], mvd,
                                   lambda: dve.wait_ge(std_s, b * 4 + (t + 1)), std[:], rstd[:], xo[:, s, :], xo_c)

        @block.scalar
        def _(act):
            with act.Fori(0, 4 * NB) as n:
                act.wait_ge(mv_s, n + 1)
                nc.scalar.activation(std[:], mv[:, 1:2], ACT.Sqrt, bias=g["eps"][:, 0:1]).then_inc(std_s, 1)

        @block.tensor
        def _(pe):
            pe.sem_inc(mm_s, 8)
            pe.wait_ge(lo_s, KD)
            with pe.Fori(0, NB) as b:
                pe.wait_ge(yl_s, b + 2)
                for t in range(4):
                    for c in range(2):
                        pe.wait_ge(rd_s, b * 8 + (2 * t + c + 1))
                        ts, cs = slice(t * P, (t + 1) * P), slice(c * 512, (c + 1) * 512)
                        three_pass(nc, bank[2 * (t % 2) + c][:], lambda k: (yh[:, k, ts], yl[:, k, ts]),
                                   lambda k: (wh[:, k, cs], wl[:, k, cs]), KD).then_inc(mm_s, 1)

        @block.gpsimd
        def _(pool):
            prime(pool, d, g, st_x)
            with pool.Fori(0, NB) as b:
                for t in range(4):
                    pool.wait_ge(xo_s, b * 4 + (t + 1))
                    pool.dma_start(d["xn1"][bass.ds(b * 512 + t * P, P), :], xo[:, t % 2, :]).then_inc(st_x[t % 2], 16)
            for s in range(2):
                pool.wait_ge(st_x[s], 16 + 32 * NB)


def phase_mlp(nc, d, g, hT, acc, half):
    NP_ = FF // P // 2
    with Box(nc, f"mlp{half}") as bx:
        raw1 = bx.sb("raw1", [P, 2, KD, P])
        w1h, w1l = bx.sb("w1h", [P, 2, KD, P], F32R), bx.sb("w1l", [P, 2, KD, P], F32R)
        raw2 = bx.sb("raw2", [P, 2, D])
        w2h, w2l = bx.sb("w2h", [P, 4, D], F32R), bx.sb("w2l", [P, 4, D], F32R)
        ah, al = bx.sb("ah", [P, 4, D], F32R), bx.sb("al", [P, 4, D], F32R)
        a = bx.sb("a", [P, 2, 512])
        b1 = bx.sb("b1", [P, FF // P])
        bank = bx.banks()
        U, V = bank[0:4], bank[4:8]
        ld_b = bx.sem("ld_b")
        ld_1, ld_2 = [bx.sem(f"ld_1{i}") for i in range(2)], [bx.sem(f"ld_2{i}") for i in range(2)]
        w1hi, w1lo, w2hi, w2lo, up_s, relu_s, sq_s, ahi_s, al_s, dn_s, acc_s = (bx.sem(n) for n in (
            "w1_hi", "w1_lo", "w2_hi", "w2_lo", "up", "relu", "sq", "a_hi", "a_lo", "down", "acc"))
        block = bx.block()

        def peeled(eng, body):
            body(0, 'u', 0)
            with eng.Fori(0, NP_ // 2 - 1) as i:
                for x, qn in (('u', 1), ('d', 0), ('u', 2), ('d', 1)):
                    body(i, x, qn)
            for x, qn in (('u', NP_ - 1), ('d', NP_ - 2), ('d', NP_ - 1)):
                body(0, x, qn)

        @block.sync
        def _(sp):
            sp.dma_start(b1[:], d["b1_col"]).then_inc(ld_b, 16)
            with sp.Fori(0, NP_) as p:
                for e in range(2):
                    sp.wait_ge(w1lo, p * 2 + (e + 1))
                    sp.dma_start(raw1[:, e], d["w1"][:, bass.ds(p * 2 * P + e * P, P)].rearrange("(k p) n -> p k n", p=P)
                                 ).then_inc(ld_1[e], 16)
                    sp.wait_ge(w2lo, p * 2 + (e + 1))
                    sp.dma_start(raw2[:, e, :], d["w2"][bass.ds(p * 2 * P + e * P, P), :]).then_inc(ld_2[e], 16)

        @block.vector
        def _(dve):
            dve.sem_inc(w1lo, 2)
            dve.sem_inc(w2lo, 2)
            dve.sem_inc(acc_s, 4)
            dve.sem_inc(al_s, 2)

            def split1(i, q):
                for e in range(2):
                    dve.wait_ge(ld_1[e], i * 32 + 16 * (q + 1))
                    if isinstance(i, int) and q == 0:
                        pass
                    else:
                        dve.wait_ge(up_s, i * 8 + (4 * q - 4 + 2 * e + 2))
                    nc.vector.tensor_copy(w1h[:, e], raw1[:, e]).then_inc(w1hi, 1)
                    dve.wait_ge(w1hi, i * 4 + (2 * q + e + 1))
                    nc.vector.tensor_tensor(w1l[:, e], raw1[:, e], w1h[:, e].bitcast(F32), ALU.subtract).then_inc(w1lo, 1)

            def split2(i, q):
                for e in range(2):
                    z = 2 * (q % 2) + e
                    dve.wait_ge(ld_2[e], i * 32 + 16 * (q + 1))
                    nc.vector.tensor_copy(w2h[:, z], raw2[:, e]).then_inc(w2hi, 1)
                    dve.wait_ge(w2hi, i * 4 + (2 * q + e + 1))
                    nc.vector.tensor_tensor(w2l[:, z], raw2[:, e], w2h[:, z].bitcast(F32), ALU.subtract).then_inc(w2lo, 1)

            def hidden(i, q):
                for e in range(2):
                    for c in range(2):
                        z, cs = 2 * (q % 2) + e, slice(c * 512, (c + 1) * 512)
                        n = 4 * q + 2 * e + c
                        dve.wait_ge(sq_s, i * 8 + (n + 1))
                        nc.vector.tensor_copy(ah[:, z, cs], a[:, c, :]).then_inc(ahi_s, 1)
                        dve.wait_ge(ahi_s, i * 8 + (n + 1))
                        nc.vector.tensor_tensor(al[:, z, cs], a[:, c, :], ah[:, z, cs].bitcast(F32), ALU.subtract).then_inc(al_s, 1)

            def gather(i, q):
                for n in range(16):
                    dve.wait_ge(dn_s, i * 32 + (16 * q + n + 1))
                    t, c = n // 2, n % 2
                    dst = acc[:, t, c * 512:(c + 1) * 512]
                    nc.vector.tensor_tensor(dst, dst, V[n % 4][:], ALU.add).then_inc(acc_s, 1)

            def body(i, x, q):
                if x == 'u':
                    hidden(i, q)
                    if not (isinstance(i, int) and q == NP_ - 1):
                        split1(i, q + 1)
                else:
                    gather(i, q)
                    if not (isinstance(i, int) and q >= NP_ - 2):
                        split2(i, q + 2)
            split1(0, 0)
            split2(0, 0)
            split2(0, 1)
            peeled(dve, body)

        @block.scalar
        def _(act):
            act.wait_ge(ld_b, 16)

            def body(i, x, q):
                if x == 'd':
                    return
                for e in range(2):
                    for c in range(2):
                        n = 4 * q + 2 * e + c
                        act.wait_ge(up_s, i * 8 + (n + 1))
                        act.wait_ge(al_s, i * 8 + (n + 1))
                        col = 2 * q + e
                        bias = b1[:, col:col + 1] if isinstance(i, int) else b1[:, bass.ds(i * 4 + col, 1)]
                        settle(act, g)
                        nc.scalar.activation(a[:, c, :], U[2 * e + c][:], ACT.Relu, bias=bias).then_inc(relu_s, 1)
                        act.wait_ge(relu_s, i * 8 + (n + 1))
                        nc.scalar.activation(a[:, c, :], a[:, c, :], ACT.Square).then_inc(sq_s, 1)
            peeled(act, body)

        @block.tensor
        def _(pe):
            def body(i, x, q):
                if x == 'u':
                    for e in range(2):
                        pe.wait_ge(w1lo, i * 4 + (2 * q + e + 1 + 2))
                        for c in range(2):
                            n = 4 * q + 2 * e + c
                            if not (isinstance(i, int) and q == 0):
                                pe.wait_ge(relu_s, i * 8 + (n - 3))
                            cs = slice(c * 512, (c + 1) * 512)
                            three_pass(nc, U[2 * e + c][:], lambda k: (w1h[:, e, k, :], w1l[:, e, k, :]),
                                       lambda k: (hT[0][:, k, cs], hT[1][:, k, cs]), KD).then_inc(up_s, 1)
                else:
                    pe.wait_ge(al_s, i * 8 + (4 * q + 4 + 2))
                    pe.wait_ge(w2lo, i * 4 + (2 * q + 2 + 2))
                    for n in range(16):
                        t, c = n // 2, n % 2
                        pe.wait_ge(acc_s, i * 32 + (16 * q + n + 1))
                        ts, cs = slice(t * P, (t + 1) * P), slice(c * 512, (c + 1) * 512)
                        z = 2 * (q % 2)
                        three_pass(nc, V[n % 4][:], lambda k: (ah[:, z + k, ts], al[:, z + k, ts]),
                                   lambda k: (w2h[:, z + k, cs], w2l[:, z + k, cs]), 2).then_inc(dn_s, 1)
            peeled(pe, body)


def phase_final(nc, d, g, acc, half):
    with Box(nc, f"fin{half}") as bx:
        xn = bx.sb("xn", [P, 2, D])
        r = bx.sb("r", [P, 2, D])
        xo = bx.sb("xo", [P, 2, D])
        ag, rb, tmp, g2, b2 = (bx.sb(n, [P, D]) for n in ("ag", "rb", "tmp", "g2", "b2"))
        stats, mv, std, rstd = bx.sb("stats", [P, 2, 6]), bx.sb("mv", [P, 2]), bx.sb("std", [P, 1]), bx.sb("rstd", [P, 1])
        ld_v = bx.sem("ld_v")
        ld_x, st_x = [bx.sem(f"ld_x{i}") for i in range(2)], [bx.sem(f"st_x{i}") for i in range(2)]
        step_s, mv_s, std_s, n_s, o_s, xr_s = (bx.sem(n) for n in ("step", "mv_done", "std", "normed", "out", "xn_read"))
        block = bx.block()
        NT = T // 2 // P
        row0 = half * (T // 2)

        @block.sync
        def _(sp):
            for dst, src in ((ag, "g1"), (rb, "b1p"), (tmp, "b_mlp2"), (g2, "g2"), (b2, "b2p")):
                sp.dma_start(dst[:], d[src].partition_broadcast(P)).then_inc(ld_v, 16)
            for t in range(NT):
                if t >= 2:
                    sp.wait_ge(xr_s, t - 1)
                sp.dma_start(xn[:, t % 2, :], d["xn1"][row0 + t * P:row0 + (t + 1) * P, :]).then_inc(ld_x[t % 2], 16)

        @block.vector
        def _(dve):
            step, xr, mvd, nrm, oc = Count(step_s), Count(xr_s), Count(mv_s), Count(n_s), Count(o_s)
            dve.wait_ge(ld_v, 80)
            step.up(nc.vector.tensor_tensor(tmp[:], tmp[:], g["mod5"][:], ALU.mult))
            step.up(nc.vector.tensor_scalar(ag[:], ag[:], ALPHA, None, ALU.mult))
            step.wait(dve)
            step.up(nc.vector.scalar_tensor_tensor(rb[:], rb[:], ALPHA, tmp[:], ALU.mult, ALU.add))
            step.wait(dve)
            for t in range(NT):
                s = t % 2
                dve.wait_ge(ld_x[s], 16 * (t // 2 + 1))
                step.up(nc.vector.tensor_tensor(xn[:, s, :], xn[:, s, :], ag[:], ALU.mult))
                step.up(nc.vector.tensor_tensor(r[:, s, :], acc[:, t, :], g["mod5"][:], ALU.mult))
                step.wait(dve)
                step.up(nc.vector.tensor_tensor(xn[:, s, :], xn[:, s, :], rb[:], ALU.add))
                step.wait(dve)
                xr.up(nc.vector.tensor_tensor(r[:, s, :], r[:, s, :], xn[:, s, :], ALU.add))
                xr.wait(dve)
                layernorm_rows(nc, g, dve, step, r[:, s, :], stats[:], mv[:], mvd,
                               lambda: dve.wait_ge(std_s, t + 1), std[:], rstd[:], r[:, s, :], nrm)
                nrm.wait(dve)
                if t >= 2:
                    dve.wait_ge(st_x[s], 16 * (t // 2))
                step.up(nc.vector.tensor_tensor(xo[:, s, :], r[:, s, :], g2[:], ALU.mult))
                step.wait(dve)
                oc.up(nc.vector.tensor_tensor(xo[:, s, :], xo[:, s, :], b2[:], ALU.add))

        @block.scalar
        def _(act):
            for t in range(NT):
                act.wait_ge(mv_s, t + 1)
                nc.scalar.activation(std[:], mv[:, 1:2], ACT.Sqrt, bias=g["eps"][:, 0:1]).then_inc(std_s, 1)

        @block.gpsimd
        def _(pool):
            for t in range(NT):
                pool.wait_ge(o_s, t + 1)
                pool.dma_start(d["out"][row0 + t * P:row0 + (t + 1) * P, :], xo[:, t % 2, :]).then_inc(st_x[t % 2], 16)
            for s in range(2):
                pool.wait_ge(st_x[s], 16 * NT // 2)


def build_program(nc, d):
    def scratch(name, shape):
        d[name] = nc.dram_tensor(f"scratch_{name}", shape, F32, kind="Internal").ap()

    scratch("pad", (16, 1, 16))
    scratch("xn", (T, D))
    scratch("xn1", (T, D))
    scratch("proj", (R_G + 2 * D, T))
    scratch("proj_ctx", (2 * BR, TC))
    scratch("u", (NTT, P, BR))
    scratch("v", (T, BR))
    scratch("v_ctx", (TC, BR))
    scratch("dft_a", (NTT, 2, P, BR))
    scratch("four", (BR, T))
    scratch("o", (2, BR, T))
    scratch("y", (D, T))

    with Box(nc, "all") as bx:
        g = {
            "ident": bx.sb("ident", [P, P]),
            "mean": bx.sb("mean", [P, P]),
            "eps": bx.sb("eps", [P, 2]),
            "scale": bx.sb("scale", [P, 3, KD]),
            "shift": bx.sb("shift", [P, 3, KD]),
            "lb": bx.sb("lb", [P, 2, H]),
            "oml": bx.sb("oml", [P, 2, H]),
            "b_in_col": bx.sb("b_in_col", [P, 40]),
            "mod2": bx.sb("mod2", [P, D]),
            "mod5": bx.sb("mod5", [P, D]),
            "primed": 0,
            "settled": bx.sem("settled"),
        }
        with Box(nc, "const") as cx:
            ld = cx.sem("ld")
            block = cx.block()

            @block.sync
            def _(sp):
                sp.dma_start(g["ident"][:], d["ident"]).then_inc(ld, 16)
                sp.dma_start(g["b_in_col"][:], d["b_in_col"]).then_inc(ld, 16)
                sp.wait_ge(ld, 32)

            @block.vector
            def _(dve):
                nc.vector.memset(g["mean"][:], 1.0 / P)
                nc.vector.memset(g["eps"][:, 0:1], LN_EPS)
                nc.vector.memset(g["eps"][:, 1:2], RMS_EPS)
        phase_vectors(nc, d, g)
        with Box(nc, "act") as ax:
            hT = (ax.sb("hTh", [P, KD, T], F32R), ax.sb("hTl", [P, KD, T], F32R))
            cT = (ax.sb("cTh", [P, KD, TC], F32R), ax.sb("cTl", [P, KD, TC], F32R))
            phase_norm_transpose(nc, d, g, "lnc", d["ctx"], 1, 2, 1, *cT)
            phase_norm_transpose(nc, d, g, "lnx", d["x"], 8, 2, 0, *hT, pos=(d["pos_row"], d["pos_col"]), xn_out=d["xn"])
            phase_project(nc, d, g, hT, cT)
            phase_project_tokens(nc, d, g, hT, cT)
        phase_fourier(nc, d, g)
        phase_hgrn(nc, d, g)
        phase_merge(nc, d, g)
        phase_out_proj(nc, d, g)
        with Box(nc, "mlp") as mx:
            acc = mx.sb("acc", [P, KD, D])
            for half in range(2):
                with Box(nc, f"mh{half}") as hx:
                    h2 = (hx.sb("h2h", [P, KD, T // 2], F32R), hx.sb("h2l", [P, KD, T // 2], F32R))
                    with Box(nc, f"z{half}") as zx:
                        block = zx.block()

                        @block.vector
                        def _(dve):
                            nc.vector.memset(acc[:], 0.0)
                    phase_norm_transpose(nc, d, g, f"ln2{half}", d["xn1"][half * (T // 2):(half + 1) * (T // 2), :], 2, 4, 2,
                                         *h2, norm=False)
                    phase_mlp(nc, d, g, h2, acc, half)
                phase_final(nc, d, g, acc, half)


def shape_constants():
    c = {"ident": np.eye(P, dtype=np.float32)}
    quarter = D // 4
    omega = (1.0 / (np.float32(10000.0) ** (np.arange(quarter, dtype=np.float32) / np.float32(quarter)))).astype(np.float32)
    r = np.arange(T // GRID_W, dtype=np.float32)[:, None] * omega
    w = np.arange(GRID_W, dtype=np.float32)[:, None] * omega
    c["pos_row"] = np.concatenate([np.sin(r), np.cos(r)], -1).astype(np.float32)
    ec = np.concatenate([np.sin(w), np.cos(w)], -1).astype(np.float32)
    c["pos_col"] = np.concatenate([ec, ec], 0)
    n1, n2, t1 = np.arange(P), np.arange(NTT), np.arange(P)
    ph = 2 * np.pi * ((t1[None, None, :] * (NTT * n1[:, None, None] + n2[None, :, None])) % T) / T
    c["dft_m1"] = np.stack([np.cos(ph), -np.sin(ph)], 2).astype(np.float32)
    p16 = 2 * np.pi * ((n2[:, None] * n2[None, :]) % NTT) / NTT
    eye8 = np.eye(8)
    bc, bs = np.kron(np.cos(p16), eye8), np.kron(np.sin(p16), eye8)
    c["dft_m2"] = np.stack([np.concatenate([bc, -bs], 1), np.concatenate([bs, bc], 1)], 1).astype(np.float32)
    pg = 2 * np.pi * ((n1[:, None] * n1[None, :]) % P) / P
    c["dft_m3"] = (np.stack([np.cos(pg), np.sin(pg)], 1) / np.sqrt(T * P)).astype(np.float32)
    m = np.zeros((P, 2, NL, H, 64), np.int32)
    s = np.arange(P)[:, None]
    t = np.arange(P)[None, :]
    for li, B in enumerate(LEVELS):
        for dr in range(2):
            later = (t // B) % 2 == 1 - dr
            ok = (s // (2 * B) == t // (2 * B)) & later & ((s // B) % 2 == dr)
            cols = np.nonzero(later[0])[0]
            m[:, dr, li] = ok[:, cols][:, None, :]
    c["masks"] = m.reshape(P, 2, NL, 256)
    c["diag"] = np.tile(np.eye(P, dtype=np.int32), (1, H))
    return c


def columns(v):
    v = np.asarray(v)
    return np.ascontiguousarray(v.reshape(v.shape[:-1] + (-1, P)).swapaxes(-1, -2))


def kernel(x, c, ctx, c_ctx, ln_in_g, ln_in_b, w_ada, b_ada, w_in, b_in, hgrn_lb_logits, hgrn_norm_g,
           w_four_proj, w_hgrn_proj, w_out, b_out, w_mlp1, b_mlp1, w_mlp2, b_mlp2, ln_post_g, ln_post_b):
    import concourse.bacc as bacc
    from concourse.bass_utils import run_bass_kernel_spmd

    A = np.asarray
    arrays = {
        "x": A(x)[0], "ctx": A(ctx)[0],
        "ccol": np.ascontiguousarray(np.stack([columns(A(c)[0]), columns(A(c_ctx))], -1)),
        "ln_in_g": A(ln_in_g), "ln_in_b": A(ln_in_b),
        "ln_cols": np.ascontiguousarray(np.stack([columns(A(ln_in_g)), columns(A(ln_in_b)), columns(A(ln_post_g)[0, 0]),
                                                  columns(A(ln_post_b)[0, 0])], 1)),
        "w_ada": A(w_ada)[0], "b_ada": A(b_ada)[0], "b_ada_col": columns(A(b_ada)[0]),
        "w_in": A(w_in)[0], "b_in": A(b_in)[0], "b_in_col": columns(A(b_in)[0]),
        "lb_logits": np.ascontiguousarray(A(hgrn_lb_logits).reshape(2, 2, H, P).transpose(3, 0, 1, 2)),
        "norm_g_col": columns(A(hgrn_norm_g)[0]),
        "w_four": A(w_four_proj)[0], "w_hgrn": A(w_hgrn_proj)[0], "w_out": A(w_out)[0], "b_out": A(b_out)[0],
        "w1": A(w_mlp1)[0], "b1_col": columns(A(b_mlp1)[0]), "w2": A(w_mlp2)[0], "b_mlp2": A(b_mlp2)[0],
        "g1": A(ln_post_g)[0, 0], "b1p": A(ln_post_b)[0, 0], "g2": A(ln_post_g)[0, 1], "b2p": A(ln_post_b)[0, 1],
    }
    arrays.update(shape_constants())
    nc = bacc.Bacc("TRN2", target_bir_lowering=False, num_devices=1)
    sent, d = {}, {}
    for name, a in arrays.items():
        a = np.ascontiguousarray(a)
        sent[f"in_{name}"] = a
        d[name] = nc.dram_tensor(f"in_{name}", a.shape, mybir.dt.from_np(a.dtype), kind="ExternalInput").ap()
    d["out"] = nc.dram_tensor("out_x", (T, D), F32, kind="ExternalOutput").ap()
    build_program(nc, d)
    r = run_bass_kernel_spmd(nc, [sent], core_ids=[0])
    return r.results[0]["out_x"].reshape(1, T, D)
```

```python
from contextlib import ExitStack, contextmanager

import numpy as np
import concourse.bass as bass
from concourse import mybir

F32 = mybir.dt.float32
F32R = mybir.dt.float32r
I32 = mybir.dt.int32
ALU = mybir.AluOpType
ACT = mybir.ActivationFunctionType

P = 128
D = 1024
T = 2048
TC = 256
BR = D // 2
H = BR // P
FF = 4 * D
KD = D // P
KB = BR // P
GRID_W = 64
NTT = T // P
LEVELS = [1, 2, 4, 8, 16, 32, 64]
NL = len(LEVELS)
ALPHA = 2.0 ** 0.25
LN_EPS = 1e-5
RMS_EPS = 1e-6
C_U, C_Q, C_V, C_FF, C_FB, C_OG, C_G = 0, BR, 2 * BR, 3 * BR, 4 * BR, 5 * BR, 6 * BR
R_F, R_Q, R_OG, R_G = 0, 2 * BR, 3 * BR, 4 * BR


class Count:

    def __init__(self, sem, credits=0):
        self.sem, self.n, self.moving = sem, credits, 0

    def up(self, ins, by=1):
        ins.then_inc(self.sem, by)
        self.n += by
        return ins

    def wait(self, eng, back=0):
        eng.wait_ge(self.sem, self.moving + (self.n - back))


@contextmanager
def repeat(eng, lo, hi, per):
    at = {c: c.n for c in per}
    with eng.Fori(lo, hi) as i:
        for c, k in per.items():
            c.moving = (i - lo) * k if lo else i * k
        yield i
    for c, k in per.items():
        assert c.n == at[c] + k, (c.sem, c.n, at[c], k)
        c.moving = 0
        c.n = at[c] + k * (hi - lo)


def settle(eng, g):
    eng.sem_inc(g["settled"], 1)


def prime(pool, d, g, sems):
    for sem in sems:
        pool.dma_start(d["pad"][g["primed"]], g["ident"][0:1, 0:16]).then_inc(sem, 16)
        g["primed"] += 1


class Box:

    def __init__(self, nc, name):
        self.nc, self.name, self.ctx, self.nums = nc, name, ExitStack(), []

    def __enter__(self):
        self.ctx.__enter__()
        return self

    def __exit__(self, *a):
        done = self.ctx.__exit__(*a)
        if self.nums and a[0] is None:
            nums = sorted(self.nums)
            with self.nc.Block() as block:
                @block.gpsimd
                def _(pool):
                    first = nums[0]
                    for n, after in zip(nums, nums[1:] + [None]):
                        if after != n + 1:
                            pool.sem_clear(range(first, n + 1))
                            first = after
        return done

    def sb(self, name, shape, dt=F32):
        return self.ctx.enter_context(self.nc.sbuf_tensor(f"{self.name}_{name}", shape, dt))

    def banks(self, n=8):
        return [self.ctx.enter_context(self.nc.psum_tensor(f"{self.name}_bank{i}", [P, 512], F32)) for i in range(n)]

    def sem(self, name):
        if name.startswith("st_"):
            return self.nc.alloc_semaphore(f"{self.name}_{name}")
        s = self.ctx.enter_context(self.nc.semaphore(f"{self.name}_{name}"))
        self.nums.append(s.num)
        return s

    def block(self):
        return self.ctx.enter_context(self.nc.Block())


def three_pass(nc, out, w, x, k_tiles):
    for k in range(k_tiles):
        (wh, wl), (xh, xl) = w(k), x(k)
        nc.tensor.matmul(out, wh, xh, start=(k == 0), stop=False)
        nc.tensor.matmul(out, wh, xl, start=False, stop=False)
        last = nc.tensor.matmul(out, wl, xh, start=False, stop=(k == k_tiles - 1))
    return last


def phase_front(nc, d, g, hT, cT):
    NG, W, NS = 1 + T // 256, 256, 3
    NH = 24
    ROWS = [4, 5, 10, 11]
    with Box(nc, "front") as bx:
        w = bx.sb("w", [P, 2, KD, 256])
        cc = bx.sb("cc", [P, KD, 2])
        sil = bx.sb("sil", [P, KD, 2])
        silb = bx.sb("silb", [P, KD, P])
        bada = bx.sb("bada", [P, 48])
        lncol = bx.sb("lncol", [P, 4, KD])
        lgt = bx.sb("lgt", [P, 2, 2, H])
        m = bx.sb("m", [P, 2, H])
        e = bx.sb("e", [P, 2, 2, H])
        ssum = bx.sb("ssum", [P, 2, H])
        mc = bx.sb("mc", [P, 48, 2])
        x = bx.sb("x", [P, NS, 2, D])
        pr = bx.sb("pr", [P, 2, BR])
        pc = bx.sb("pc", [P, 1, BR])
        hf = bx.sb("hf", [P, 2, W])
        stats, mv = bx.sb("stats", [P, 2, 2, 6]), bx.sb("mv", [P, 2, 2])
        std, rstd = bx.sb("std", [P, 2]), bx.sb("rstd", [P, 2])
        bank = bx.banks()
        TR, COL, ROW = bank[0:5], bank[5:7], bank[7]
        ld_small, ld_w, ld_c = bx.sem("ld_small"), [bx.sem(f"ld_w{i}") for i in range(2)], bx.sem("ld_c")
        ld_x, ld_p, ld_row = [bx.sem(f"ld_x{i}") for i in range(NS)], bx.sem("ld_p"), bx.sem("ld_row")
        st_x = [bx.sem(f"st_x{i}") for i in range(NS)]
        silu_s, silb_s, step_s, exp_s, half_s, row_s, mod_s, mv_s, std_s, xn_s, xT, evac, hi_s, split = (bx.sem(n) for n in (
            "silu", "silb", "step", "exp", "half_done", "row_read", "mod_ready", "mv_done", "std", "xn_ready", "xT",
            "evac", "h_hi", "h_split"))
        block = bx.block()

        def stored(n):
            return 16 * (n // NS + (1 if n % NS else 0))

        @block.sync
        def _(sp):
            for dst, src in ((cc[:], d["ccol"]), (bada[:], d["b_ada_col"]), (lncol[:], d["ln_cols"]), (lgt[:], d["lb_logits"])):
                sp.dma_start(dst, src).then_inc(ld_small, 16)
            for hh in range(NH):
                if hh >= 2:
                    sp.wait_ge(half_s, hh - 1)
                sp.dma_start(w[:, hh % 2], d["w_ada"][:, hh * 256:(hh + 1) * 256].rearrange("(k p) n -> p k n", p=P)
                             ).then_inc(ld_w[hh % 2], 16)
                if hh == 1:
                    sp.dma_start(pc[:, 0, :], d["pos_col"]).then_inc(ld_c, 16)
                    for name, c in (("mod2", 2), ("mod5", 5)):
                        sp.dma_start(g[name][:], d["b_ada"][c * D:(c + 1) * D].partition_broadcast(P)).then_inc(ld_row, 16)

        @block.scalar
        def _(act):
            def load(n):
                if n >= NS:
                    act.wait_ge(xT, KD * (n - NS + 1))
                    if n > NS:
                        act.wait_ge(st_x[n % NS], stored(n - NS))
                src = d["ctx"] if n == 0 else d["x"][(n - 1) * W:n * W, :]
                act.dma_start(x[:, n % NS], src.rearrange("(s p) n -> p s n", p=P)).then_inc(ld_x[n % NS], 16)

            def load_rows(n):
                er = d["pos_row"].rearrange("(r h) n -> h r n", h=2)
                for h in range(2):
                    act.dma_start(pr[64 * h:64 * h + 64], er[h, 2 * (n - 1):2 * n, :].partition_broadcast(64)).then_inc(ld_p, 16)

            def root(n):
                act.wait_ge(mv_s, n + 1)
                nc.scalar.activation(std[:], mv[:, :, 1], ACT.Sqrt, bias=g["eps"][:, 0:1]).then_inc(std_s, 1)
                if n + 1 < NG and n > 0:
                    load_rows(n + 1)
            for n in range(NS):
                load(n)
            load_rows(1)
            act.wait_ge(ld_small, 64)
            nc.scalar.activation(sil[:], cc[:], ACT.Silu).then_inc(silu_s, 1)
            act.wait_ge(step_s, 3)
            nc.scalar.activation(e[:], e[:], ACT.Exp).then_inc(exp_s, 1)
            root(0)
            for n in range(NG):
                if n + 1 < NG:
                    root(n + 1)
                if n == 0:
                    act.wait_ge(mod_s, 1)
                which = 1 if n == 0 else 0
                for k in range(KD):
                    t = n * KD + k
                    act.wait_ge(xT, t + 1)
                    if t >= 2:
                        act.wait_ge(split, t - 1)
                    nc.scalar.activation(hf[:, k % 2, :], TR[t % 5][:, 0:W], ACT.Identity, bias=g["shift"][:, which, k:k + 1],
                                         scale=g["scale"][:, which, k:k + 1]).then_inc(evac, 1)
                if n + NS < NG:
                    load(n + NS)

        @block.tensor
        def _(pe):
            pe.wait_ge(silu_s, 1)
            pe.wait_ge(silb_s, 1)

            def chunk(j):
                for half in range(2):
                    hh = 2 * j + half
                    pe.wait_ge(ld_w[hh % 2], 16 * (hh // 2 + 1))
                    if j in ROWS:
                        if half == 0 and j != ROWS[0]:
                            pe.wait_ge(row_s, ROWS.index(j))
                        for k in range(KD):
                            last = nc.tensor.matmul(ROW[:, half * 256:half * 256 + 256], silb[:, k, :], w[:, hh % 2, k, :],
                                                    start=(k == 0), stop=(k == KD - 1))
                    else:
                        out = COL[0 if j < 4 else 1]
                        for mt in range(2):
                            col = (2 * hh + mt) * 2
                            for k in range(KD):
                                last = nc.tensor.matmul(out[:, col:col + 2], w[:, hh % 2, k, mt * P:(mt + 1) * P],
                                                        sil[:, k, :], start=(k == 0), stop=(k == KD - 1))
                    last.then_inc(half_s, 1)
            for j in range(4):
                chunk(j)
            for n in range(NG):
                pe.wait_ge(xn_s, n + 1)
                for k in range(KD):
                    t = n * KD + k
                    if t >= 5:
                        pe.wait_ge(evac, t - 4)
                    for s in range(2):
                        last = nc.tensor.transpose(TR[t % 5][:, s * P:(s + 1) * P], x[:, n % NS, s, k * P:(k + 1) * P], g["ident"][:])
                    last.then_inc(xT, 1)
                if n:
                    chunk(3 + n)

        @block.vector
        def _(dve):
            step = Count(step_s)

            def bounds():
                step.up(nc.vector.tensor_tensor(m[:], lgt[:, :, 0, :], lgt[:, :, 1, :], ALU.max))
                step.wait(dve)
                for i in range(2):
                    step.up(nc.vector.tensor_tensor(e[:, :, i, :], lgt[:, :, i, :], m[:], ALU.subtract))
                dve.wait_ge(silu_s, 1)
                nc.vector.tensor_copy(silb[:], sil[:, :, 0:1].to_broadcast([P, KD, P])).then_inc(silb_s, 1)
                dve.wait_ge(exp_s, 1)
                step.up(nc.vector.tensor_tensor(ssum[:], e[:, :, 0, :], e[:, :, 1, :], ALU.add))
                step.wait(dve)
                step.up(nc.vector.reciprocal(m[:], ssum[:]))
                step.wait(dve)
                step.up(nc.vector.tensor_tensor(g["lb"][:], e[:, :, 0, :], m[:], ALU.mult))
                step.wait(dve)
                step.up(nc.vector.tensor_scalar(g["oml"][:], g["lb"][:], -1.0, 1.0, ALU.mult, ALU.add))

            def columns_ready(bank_, a, b, parts):
                step.up(nc.vector.tensor_tensor(mc[:, a:b, :], bank_[:, 2 * a:2 * b].rearrange("p (a b) -> p a b", b=2),
                                                bada[:, a:b].rearrange("p (a b) -> p a b", b=1).to_broadcast([P, b - a, 2]), ALU.add))
                step.wait(dve)
                for i, who, sh, lng in parts:
                    sc, bi = g["scale"][:, i, :], g["shift"][:, i, :]
                    one = mc[:, (sh + 1) * 8:(sh + 2) * 8, who]
                    step.up(nc.vector.scalar_tensor_tensor(sc, one, 1.0, lncol[:, lng, :], ALU.add, ALU.mult))
                    step.up(nc.vector.scalar_tensor_tensor(bi, one, 1.0, lncol[:, lng + 1, :], ALU.add, ALU.mult))
                    step.wait(dve)
                    step.up(nc.vector.tensor_tensor(bi, bi, mc[:, sh * 8:(sh + 1) * 8, who], ALU.add))

            def normalise(n):
                xs = x[:, n % NS]
                dve.wait_ge(ld_x[n % NS], 16 * (n // NS + 1))
                if n:
                    dve.wait_ge(ld_p, 32 * n)
                    step.up(nc.vector.tensor_tensor(xs[:, :, 0:BR], xs[:, :, 0:BR], pr[:], ALU.add))
                    step.up(nc.vector.tensor_tensor(xs[:, :, BR:D], xs[:, :, BR:D], pc[:].to_broadcast([P, 2, BR]), ALU.add))
                    step.wait(dve)
                for s in range(2):
                    for c in range(2):
                        step.up(nc.vector.bn_stats(stats[:, s, c, :], xs[:, s, c * 512:(c + 1) * 512]))
                step.wait(dve)
                step.up(nc.vector.bn_aggr(mv[:, 0, :], stats[:, 0].rearrange("p a b -> p (a b)")))
                nc.vector.bn_aggr(mv[:, 1, :], stats[:, 1].rearrange("p a b -> p (a b)")).then_inc(mv_s, 1)
                dve.wait_ge(std_s, n + 1)
                step.up(nc.vector.reciprocal(rstd[:], std[:]))
                step.wait(dve)
                for s in range(2):
                    last = nc.vector.tensor_scalar(xs[:, s, :], xs[:, s, :], mv[:, s, 0:1], rstd[:, s:s + 1], ALU.subtract, ALU.mult)
                    if s == 0:
                        step.up(last)
                last.then_inc(xn_s, 1)

            def row_chunk(c):
                j = 3 + c
                if j in ROWS:
                    dst = g["mod2" if j < 8 else "mod5"][:, (j % 2) * 512:(j % 2) * 512 + 512]
                    dve.wait_ge(ld_row, 32)
                    dve.wait_ge(half_s, 2 * (j + 1))
                    nc.vector.tensor_tensor(dst, dst, ROW[:], ALU.add).then_inc(row_s, 1)
            dve.wait_ge(ld_small, 64)
            bounds()
            normalise(0)
            dve.wait_ge(ld_c, 16)
            for n in range(NG):
                if n + 1 < NG:
                    normalise(n + 1)
                if n == 0:
                    dve.wait_ge(half_s, 8)
                    columns_ready(COL[0], 0, 16, ((0, 0, 0, 0), (1, 1, 0, 0)))
                    step.wait(dve)
                    dve.sem_inc(mod_s, 1)
                to, c0 = (cT, 0) if n == 0 else (hT, (n - 1) * W)
                for k in range(KD):
                    t = n * KD + k
                    hi = to[0][:, k, c0:c0 + W]
                    dve.wait_ge(evac, t + 1)
                    nc.vector.tensor_copy(hi, hf[:, k % 2, :]).then_inc(hi_s, 1)
                    dve.wait_ge(hi_s, t + 1)
                    nc.vector.tensor_tensor(to[1][:, k, c0:c0 + W], hf[:, k % 2, :], hi.bitcast(F32), ALU.subtract).then_inc(split, 1)
                if n >= 2:
                    row_chunk(n - 1)
            row_chunk(NG - 1)
            dve.wait_ge(half_s, 20)
            columns_ready(COL[1], 24, 40, ((2, 0, 3, 2),))

        @block.gpsimd
        def _(pool):
            for n in range(1, NG):
                pool.wait_ge(xn_s, n + 1)
                pool.dma_start(d["xn"][(n - 1) * W:n * W, :].rearrange("(s p) n -> p s n", p=P), x[:, n % NS]).then_inc(st_x[n % NS], 16)
            for s in range(NS):
                pool.wait_ge(st_x[s], stored(NG - NS + s))


def phase_project(nc, d, g, hT, cT):
    secs = [(C_FF, 8, ACT.Sigmoid, "ctx", 0, True),
            (C_FF, 8, ACT.Sigmoid, "lat", R_F, True),
            (C_G, 16, ACT.Sigmoid, "lat", R_G, False),
            (C_Q, 4, ACT.Silu, "lat", R_Q, False),
            (C_OG, 4, ACT.Silu, "lat", R_OG, False)]
    with Box(nc, "proj") as bx:
        raw = bx.sb("raw", [P, 2, KD, P])
        wh = bx.sb("wh", [P, 2, KD, P], F32R)
        wl = bx.sb("wl", [P, 2, KD, P], F32R)
        stage = bx.sb("stage", [P, 2, T])
        bank = bx.banks()
        ld_w = [bx.sem(f"ld_w{i}") for i in range(2)]
        st_o = [bx.sem(f"st_o{i}") for i in range(2)]
        w_hi, w_split, strip_done, mm_done, evac, f_done = (bx.sem(n) for n in (
            "w_hi", "w_split", "strip_done", "mm_done", "evac", "f_done"))
        block = bx.block()
        lbv = g["lb"][:].rearrange("p a b -> p (a b)")
        omv = g["oml"][:].rearrange("p a b -> p (a b)")

        @block.sync
        def _(sp):
            n0 = 0
            for col, n, _, _, _, _ in secs:
                with sp.Fori(0, n // 2) as i:
                    for s in range(2):
                        sp.wait_ge(w_split, i * 2 + (n0 + s + 1))
                        sp.dma_start(raw[:, s], d["w_in"][:, bass.ds(i * 2 * P + (col + s * P), P)].rearrange("(k p) n -> p k n", p=P)
                                     ).then_inc(ld_w[s], 16)
                n0 += n

        @block.vector
        def _(dve):
            dve.sem_inc(w_split, 2)
            n0 = 0
            for _, n, _, _, _, _ in secs:
                with dve.Fori(0, n // 2) as i:
                    for s in range(2):
                        dve.wait_ge(ld_w[s], i * 16 + (n0 * 8 + 16))
                        dve.wait_ge(strip_done, i * 2 + (n0 + s + 1))
                        nc.vector.tensor_copy(wh[:, s], raw[:, s]).then_inc(w_hi, 1)
                        dve.wait_ge(w_hi, i * 2 + (n0 + s + 1))
                        nc.vector.tensor_tensor(wl[:, s], raw[:, s], wh[:, s].bitcast(F32), ALU.subtract).then_inc(w_split, 1)
                n0 += n

        @block.tensor
        def _(pe):
            pe.sem_inc(strip_done, 2)
            n0 = 0
            ev0 = 0
            for col, n, _, who, _, _ in secs:
                nch, W = (4, 512) if who == "lat" else (1, TC)
                hi, lo = hT if who == "lat" else cT
                if ev0 == 8:
                    pe.wait_ge(evac, ev0 + 8)
                with pe.Fori(0, n // 2) as i:
                    for s in range(2):
                        pe.wait_ge(w_split, i * 2 + (n0 + s + 3))
                        for c in range(nch):
                            pe.wait_ge(evac, i * 2 * nch + (ev0 + s * nch + c + 1 + (0 if nch == 4 else 6)))
                            out = bank[(4 * s + c)][:, 0:W]
                            last = three_pass(nc, out, lambda k: (wh[:, s, k, :], wl[:, s, k, :]),
                                              lambda k: (hi[:, k, c * W:(c + 1) * W], lo[:, k, c * W:(c + 1) * W]), KD)
                            last.then_inc(mm_done, 1)
                        pe.wait_ge(mm_done, i * 2 * nch + (ev0 + (s + 1) * nch))
                        pe.sem_inc(strip_done, 1)
                n0 += n
                ev0 += n * nch

        @block.scalar
        def _(act):
            act.sem_inc(evac, 8)
            n0 = 0
            ev0 = 0
            for col, n, func, who, row, _ in secs:
                nch, W = (4, 512) if who == "lat" else (1, TC)
                with act.Fori(0, n // 2) as i:
                    for s in range(2):
                        act.wait_ge(st_o[s], i * 16 + (n0 * 8 + 16))
                        for c in range(nch):
                            act.wait_ge(mm_done, i * 2 * nch + (ev0 + s * nch + c + 1))
                            settle(act, g)
                            nc.scalar.activation(stage[:, s, c * W:(c + 1) * W], bank[4 * s + c][:, 0:W], func,
                                                 bias=g["b_in_col"][:, bass.ds(i * 2 + (col // P + s), 1)]).then_inc(evac, 1)
                n0 += n
                ev0 += n * nch

        @block.gpsimd
        def _(pool):
            n0 = 0
            ev0 = 0
            fdone = 0
            prime(pool, d, g, st_o)
            for col, n, _, who, row, is_f in secs:
                nch, W = (4, 512) if who == "lat" else (1, TC)
                dst = d["proj"] if who == "lat" else d["proj_ctx"]
                if is_f:
                    for m in range(n):
                        part = stage[:, m % 2, 0:nch * W]
                        pool.wait_ge(evac, ev0 + (m + 1) * nch + 8)
                        nc.gpsimd.tensor_scalar(part, part, omv[:, m:m + 1], lbv[:, m:m + 1], ALU.mult, ALU.add).then_inc(f_done, 1)
                        fdone += 1
                        pool.wait_ge(f_done, fdone)
                        pool.dma_start(dst[row + m * P:row + (m + 1) * P, :], part).then_inc(st_o[m % 2], 16)
                else:
                    with pool.Fori(0, n // 2) as i:
                        for s in range(2):
                            pool.wait_ge(evac, i * 2 * nch + (ev0 + (s + 1) * nch + 8))
                            pool.dma_start(dst[bass.ds(i * 2 * P + (row + s * P), P), :], stage[:, s, 0:nch * W]).then_inc(st_o[s], 16)
                n0 += n
                ev0 += n * nch
            for s in range(2):
                pool.wait_ge(st_o[s], 16 + 8 * n0)


def phase_project_tokens(nc, d, g, hT, cT):
    with Box(nc, "tok") as bx:
        raw = bx.sb("raw", [P, 2, BR])
        wh = bx.sb("wh", [P, KD, BR], F32R)
        wl = bx.sb("wl", [P, KD, BR], F32R)
        stage = bx.sb("stage", [P, 4, BR])
        brow = bx.sb("brow", [P, 2, BR])
        bank = bx.banks()
        ld_b, ld_w = bx.sem("ld_b"), [bx.sem(f"ld_w{i}") for i in range(2)]
        st_o = [bx.sem(f"st_o{i}") for i in range(4)]
        w_hi, w_split, w_used, mm_done, evac = (bx.sem(n) for n in ("w_hi", "w_split", "w_used", "mm_done", "evac"))
        block = bx.block()
        jobs = [(0, hT, n2, NTT, d["u"][n2]) for n2 in range(NTT)]
        jobs += [(1, cT, t * P, 1, d["v_ctx"][t * P:(t + 1) * P, :]) for t in range(TC // P)]
        jobs += [(1, hT, t * P, 1, d["v"][t * P:(t + 1) * P, :]) for t in range(NTT)]
        first_v = NTT

        @block.sync
        def _(sp):
            for i, c in enumerate((C_U, C_V)):
                sp.dma_start(brow[:, i, :], d["b_in"][c:c + BR].partition_broadcast(P)).then_inc(ld_b, 16)
            for n in range(2 * KD):
                if n >= 2:
                    sp.wait_ge(w_split, n - 1)
                c, k = (C_U, C_V)[n // KD], n % KD
                sp.dma_start(raw[:, n % 2, :], d["w_in"][k * P:(k + 1) * P, c:c + BR]).then_inc(ld_w[n % 2], 16)

        @block.vector
        def _(dve):
            def split(sec, k):
                n = sec * KD + k
                dve.wait_ge(ld_w[n % 2], 16 * (n // 2 + 1))
                if sec and k < KD - 1:
                    dve.wait_ge(w_used, k + 1)
                elif sec:
                    dve.wait_ge(mm_done, first_v)
                nc.vector.tensor_copy(wh[:, k, :], raw[:, n % 2, :]).then_inc(w_hi, 1)
                dve.wait_ge(w_hi, n + 1)
                nc.vector.tensor_tensor(wl[:, k, :], raw[:, n % 2, :], wh[:, k, :].bitcast(F32), ALU.subtract).then_inc(w_split, 1)
            for k in range(KD):
                split(0, k)
            dve.wait_ge(ld_b, 32)
            for n, (sec, _, _, _, _) in enumerate(jobs):
                if n == first_v - 8:
                    for k in range(KD - 1):
                        split(1, k)
                if n == first_v:
                    split(1, KD - 1)
                dve.wait_ge(mm_done, n + 1)
                if n >= 4:
                    dve.wait_ge(st_o[n % 4], 16 * (n // 4))
                nc.vector.tensor_tensor(stage[:, n % 4, :], bank[n % 8][:], brow[:, sec, :], ALU.add).then_inc(evac, 1)

        @block.tensor
        def _(pe):
            def product(n, k):
                sec, (hi, lo), t0, st, _ = jobs[n]
                sl = slice(t0, t0 + st * (P - 1) + 1, st)
                if k == 0 and n >= 8:
                    pe.wait_ge(evac, n - 7)
                nc.tensor.matmul(bank[n % 8][:], hi[:, k, sl], wh[:, k, :], start=(k == 0), stop=False)
                nc.tensor.matmul(bank[n % 8][:], hi[:, k, sl], wl[:, k, :], start=False, stop=False)
                last = nc.tensor.matmul(bank[n % 8][:], lo[:, k, sl], wh[:, k, :], start=False, stop=(k == KD - 1))
                if k == KD - 1:
                    last.then_inc(mm_done, 1)
                return last
            for n0 in range(0, first_v + 8, 8):
                for k in range(KD):
                    if n0 != first_v - 8:
                        pe.wait_ge(w_split, KD * (n0 // first_v) + k + 1)
                    for n in range(n0, n0 + 8):
                        last = product(n, k)
                    if n0 == first_v - 8 and k < KD - 1:
                        last.then_inc(w_used, 1)
            for n in range(first_v + 8, len(jobs)):
                for k in range(KD):
                    product(n, k)

        @block.gpsimd
        def _(pool):
            for n, job in enumerate(jobs):
                pool.wait_ge(evac, n + 1)
                pool.dma_start(job[4], stage[:, n % 4, :]).then_inc(st_o[n % 4], 16)
            for s in range(4):
                pool.wait_ge(st_o[s], 16 * len(range(s, len(jobs), 4)))


def phase_mix(nc, d, g):
    NU, NX, HP, W2 = 2 * NTT, TC // P, H * P, 2 * H * P
    SL = 4
    X = 2 * NX
    with Box(nc, "mix") as bx:
        w = bx.sb("w", [P, 2, 2, 2, HP])
        qk = bx.sb("qk", [P, 2, 2, 2, HP])
        v = bx.sb("v", [P, 2, 2, BR])
        lev = bx.sb("lev", [P, 2, NL, HP])
        qkd = bx.sb("qkd", [P, 2, 2, HP])
        pm = bx.sb("pm", [P, 2, HP])
        kdT = bx.sb("kdT", [P, 2, HP])
        st = bx.sb("st", [P, 2, HP])
        ost = bx.sb("ost", [P, 2, HP])
        mask = bx.sb("mask", [P, 2, NL - 1, 256], I32)
        diag = bx.sb("diag", [P, HP], I32)
        m1 = bx.sb("m1", [P, 2, 2, P])
        u_in = bx.sb("u_in", [P, 2, BR])
        a_st = bx.sb("a_st", [P, 2, 2, BR])
        m2 = bx.sb("m2", [P, 2, 2 * P])
        m3 = bx.sb("m3", [P, 2, P])
        xin = bx.sb("xin", [P, 2, 2, SL, P])
        zT = bx.sb("zT", [P, 2, 2, 512])
        fst = bx.sb("fst", [P, T])
        bank = bx.banks()
        SC, DG, TO, SS, FT = bank[0:4], bank[4], bank[5], bank[6], bank[7]
        ld_m = bx.sem("ld_m")
        ld = [[bx.sem(f"ld_{x}{s}") for s in range(2)] for x in "fb"]
        ld_n = [bx.sem(f"ld_n{i}") for i in range(2)]
        st_o, st_a = ([bx.sem(f"st_{n}{i}") for i in range(2)] for n in ("o", "a"))
        st_f = bx.sem("st_f")
        ld_x = [bx.sem(f"st_x{i}") for i in range(2)]
        step_s, ready, kk_done, ones, scores, masked, m64, trans, trcopy, o_mm, o_out, s_mm, s_new, f_mm, f_out = (
            bx.sem(n) for n in ("step", "lev_ready", "kk_done", "ones", "scores", "masked", "m64", "trans", "trcopy",
                                "o_mm", "o_out", "s_mm", "s_new", "f_mm", "f_out"))
        block = bx.block()
        ad = d["dft_a"]

        F2 = 2 * 16 - 12 * 4

        def at(i, k, per, c):
            return i * (SL * per) + (k * per + c)

        def halves(ap, B):
            return ap.rearrange("p (m two b) -> p m two b", two=2, b=B)

        def key_half(dr):
            return dr

        def halves_of(buf, dr, s, B):
            t = buf[:, dr, s]
            off, row = t.offset, t.ap[0]
            if key_half(dr) == 0:
                return bass.AP(t.tensor, off, [row, [2 * B, 256 // B], [HP + B, 2], [1, B]])
            return bass.AP(t.tensor, off + HP + B, [row, [2 * B, 256 // B], [-(HP + B), 2], [1, B]])

        def other_total(dr, s, B):
            t = w[:, dr, s]
            kh, e = key_half(dr), (B - 1 if dr == 0 else 0)
            pre = t.offset + (1 - kh) * HP
            first = pre + (1 - kh) * B + e
            stp = (kh - (1 - kh)) * B
            return bass.AP(t.tensor, first, [t.ap[0], [2 * B, 256 // B], [stp, 2], [0, B]])

        def out_halves(buf, dr, B):
            t = halves(buf, B)
            return t if key_half(dr) == 0 else t[:, :, ::-1]

        def pre_of(dr, s):
            return w[:, dr, s, 1 - key_half(dr)]

        def run(eng, slot):
            for k in range(SL):
                slot(0, k, 1)
            with eng.Fori(1, 4) as i:
                for k in range(SL):
                    slot(i, k, 1)
            with eng.Fori(4, NU // SL - 1) as i:
                for k in range(SL):
                    slot(i, k, 2)
            for k in range(SL):
                slot(NU // SL - 1, k, 2)

        @block.sync
        def _(sp):
            for j in range(NX):
                for dr in range(2):
                    c = j * P if dr == 0 else (NX - 1 - j) * P
                    sp.dma_start(pre_of(dr, j % 2), d["proj_ctx"][dr * BR:(dr + 1) * BR, c:c + P].rearrange("(h p) t -> p h t", p=P)
                                 ).then_inc(ld[dr][j % 2], 16)
                    sp.dma_start(v[:, dr, j % 2, :], d["v_ctx"][c:c + P, :]).then_inc(ld[dr][j % 2], 16)
            for dst, src in ((mask, "masks"), (diag, "diag"), (m2, "dft_m2"), (m3, "dft_m3")):
                sp.dma_start(dst[:], d[src]).then_inc(ld_m, 16)

            def slot(i, k, part):
                s, dr = k // 2, k % 2
                sp.wait_ge(s_new, at(i, k, 1, 1))
                base = (P * s) if dr == 0 else ((NTT - 1 - s) * P)
                c = i * (2 * P if dr == 0 else -2 * P) + base
                cs = slice(c, c + P) if isinstance(c, int) else bass.ds(c, P)
                pf = d["proj"][R_F + dr * BR:R_F + (dr + 1) * BR, :]
                pq = d["proj"][R_Q:R_Q + BR, :]
                sp.dma_start(pre_of(dr, s), pf[:, cs].rearrange("(h p) t -> p h t", p=P)).then_inc(ld[dr][s], 16)
                sp.dma_start(qk[:, dr, s, 1 - key_half(dr)], pq[:, cs].rearrange("(h p) t -> p h t", p=P)).then_inc(ld[dr][s], 16)
                sp.dma_start(v[:, dr, s, :], d["v"][cs, :]).then_inc(ld[dr][s], 16)
                if part == 1:
                    if not (isinstance(i, int) and i == 0 and k < 2):
                        sp.wait_ge(f_mm, at(i, k, 2, -2))
                    n = slice(k, k + 1) if isinstance(i, int) else bass.ds(i * SL + k, 1)
                    sp.dma_start(u_in[:, k % 2, :], d["u"][n].rearrange("n p c -> p (n c)")).then_inc(ld_n[k % 2], 16)
                    sp.dma_start(m1[:, k % 2], d["dft_m1"][n].rearrange("n p r c -> p (n r) c")).then_inc(ld_n[k % 2], 16)
            run(sp, slot)

        @block.vector
        def _(dve):
            step = Count(step_s)
            per_u = 1 + 7 * 2

            def gates(i, k, latent, between=lambda n: None):
                s, dr = k // 2, k % 2
                for li, B in enumerate(LEVELS):
                    ww = halves_of(w, dr, s, B)
                    if latent:
                        nc.vector.tensor_tensor(out_halves(lev[:, dr, li], dr, B), halves_of(qk, dr, s, B), ww, ALU.mult
                                                ).then_inc(ready, 1)
                        between(2 * li)
                        dve.wait_ge(ready, at(i, k, NL + 1, X + li + 1))
                    step.up(nc.vector.tensor_tensor(ww, ww, other_total(dr, s, B), ALU.mult))
                    between(2 * li + 1)
                    step.wait(dve)

            def whole(dr, s, latent):
                if latent:
                    src, dst, m = qk[:, dr, s], qkd[:, dr], w[:, dr, s]
                else:
                    kp = key_half(dr)
                    src, dst, m = qk[:, dr, s, kp], qkd[:, dr, kp], w[:, dr, s, kp]
                nc.vector.tensor_tensor(dst, src, m, ALU.mult).then_inc(ready, 1)

            def new_state(i, k):
                s, dr = k // 2 % 2, k % 2
                dve.wait_ge(s_mm, at(i, k, 1, X + 1))
                e = P - 1 if dr == 0 else 0
                for h in range(H):
                    c = slice(h * P, (h + 1) * P)
                    last = nc.vector.scalar_tensor_tensor(st[:, dr, c], st[:, dr, c],
                                                          pre_of(dr, s)[:, h * P + e:h * P + e + 1], SS[:, c], ALU.mult, ALU.add)
                    if h < H - 1:
                        step.up(last)
                last.then_inc(s_new, 1)

            def mask_score(i, k, n):
                dr = k % 2
                dve.wait_ge(scores, at(i, k, 5, (1, 1, 2, 2, 3, 3, 5)[n]))
                if n:
                    dve.wait_ge(masked, at(i, k, NL, n))
                settle(dve, g)
                if n < NL - 1:
                    B = LEVELS[n]
                    nc.vector.copy_predicated(halves(pm[:, dr], B)[:, :, 1 - key_half(dr)],
                                              mask[:, dr, n].rearrange("p (m b) -> p m b", b=B),
                                              SC[n // 2][:, (n % 2) * 256:(n % 2) * 256 + 256].rearrange("p (m b) -> p m b", b=B)
                                              ).then_inc(masked, 1)
                else:
                    nc.vector.copy_predicated(pm[:, dr], diag[:], DG[:]).then_inc(masked, 1)

            def prepare(i, k, between=lambda n: None):
                s, dr = k // 2, k % 2
                dve.wait_ge(ld[dr][s], i * 48 + (32 * (NX // 2) + 48))
                dve.wait_ge(kk_done, at(i, k, 1, X + 1))
                dve.wait_ge(ones, at(i, k, 1, X + 1))
                gates(i, k, True, between)

            step.up(nc.vector.memset(st[:], 0.0))
            step.up(nc.vector.memset(pm[:], 0.0))
            for n in range(X):
                s, dr = n // 2 % 2, n % 2
                dve.wait_ge(ld[dr][s], 32 * (n // 4 + 1))
                dve.wait_ge(kk_done, n + 1)
                dve.wait_ge(ones, n + 1)
                gates(0, n, False)
                whole(dr, s, False)
                if n:
                    new_state(-1, n - 1)
            prepare(0, 0)
            whole(0, 0, True)
            new_state(-1, X - 1)
            dve.wait_ge(ld_m, 64)

            def slot(i, k, part):
                last = isinstance(i, int) and i == NU // SL - 1 and k == SL - 1
                ni, nk = (i, k + 1) if k < SL - 1 else (i + 1, 0)

                def between(n):
                    if n >= 5 and n - 5 < NL:
                        mask_score(i, k, n - 5)
                if not last:
                    prepare(ni, nk, between)
                    done = 2 * NL - 5
                else:
                    done = 0
                for n in range(min(done, NL), NL):
                    mask_score(i, k, n)
                if not (isinstance(i, int) and i == 0 and k == 0):
                    pi, pk = (i, k - 1) if k else (i - 1, SL - 1)
                    new_state(pi, pk)
                if not last:
                    whole(nk % 2, nk // 2, True)
            for k in range(SL):
                slot(0, k, 1)
            per = SL * (NL + H - 1)
            with repeat(dve, 1, NU // SL - 1, {step: per}) as i:
                for k in range(SL):
                    slot(i, k, 1)
            for k in range(SL):
                slot(NU // SL - 1, k, 2)

        @block.tensor
        def _(pe):
            def transpose_keys(dr, n):
                for h in range(H):
                    last = nc.tensor.transpose(TO[:, h * P:(h + 1) * P], qkd[:, dr, key_half(dr), h * P:(h + 1) * P], g["ident"][:])
                last.then_inc(trans, 1)

            def state_product(dr, s):
                for h in range(H):
                    c = slice(h * P, (h + 1) * P)
                    last = nc.tensor.matmul(SS[:, c], kdT[:, dr, c], v[:, dr, s, c], start=True, stop=True)
                last.then_inc(s_mm, 1)

            def fourier(i, k, part, piece):
                if part == 1:
                    pe.wait_ge(ld_n[k % 2], i * 64 + 32 * (k // 2 + 1))
                    pe.wait_ge(f_out, at(i, k, 2, piece + 1))
                    nc.tensor.matmul(FT[:], m1[:, k % 2, piece, :], u_in[:, k % 2, :], start=True, stop=True).then_inc(f_mm, 1)
                else:
                    pe.wait_ge(ld_x[k % 2], i * 64 + (32 * (k // 2 + 1) - 64 * 4))
                    pe.wait_ge(f_out, i * 12 + (F2 + 3 * k + piece + 1))
                    for x in range(2):
                        for r in range(2):
                            last = nc.tensor.matmul(FT[:, x * 256:(x + 1) * 256], xin[:, k % 2, r, 2 * piece + x, :], m2[:, r, :],
                                                    start=(r == 0), stop=(r == 1))
                    last.then_inc(f_mm, 1)

            def channels(i, k):
                pe.wait_ge(f_out, i * 12 + (F2 + 3 * k + 2 + 1))
                for r in range(2):
                    last = nc.tensor.matmul(FT[:], m3[:, r, :], zT[:, k % 2, r, :], start=(r == 0), stop=(r == 1))
                last.then_inc(f_mm, 1)

            for n in range(X):
                pe.wait_ge(ready, n + 1)
                if n:
                    pe.wait_ge(trcopy, n)
                transpose_keys(n % 2, n)
                pe.wait_ge(trcopy, n + 1)
                if n:
                    pe.wait_ge(s_new, n)
                state_product(n % 2, n // 2 % 2)

            def output(i, k):
                s, dr = k // 2, k % 2
                pe.wait_ge(s_new, at(i, k, 1, X - 1))
                for h in range(H):
                    c = slice(h * P, (h + 1) * P)
                    nc.tensor.matmul(TO[:, c], v[:, dr, s, c], pm[:, dr, c], start=True, stop=False)
                    last = nc.tensor.matmul(TO[:, c], st[:, dr, c], qkd[:, dr, 1 - key_half(dr), c], start=False, stop=True)
                last.then_inc(o_mm, 1)
                pe.wait_ge(s_new, at(i, k, 1, X))
                state_product(dr, s)

            def slot(i, k, part):
                dr = k % 2
                first = isinstance(i, int) and i == 0 and k == 0
                if not first:
                    pe.wait_ge(masked, at(i, k, NL, 0))
                for li, B in enumerate(LEVELS):
                    pe.wait_ge(ready, at(i, k, NL + 1, X + li + 1))
                    if li == NL - 1 and not first:
                        pe.wait_ge(m64, at(i, k, 1, 0))
                    for h in range(H):
                        lv = lev[:, dr, li, h * P:(h + 1) * P]
                        last = nc.tensor.matmul(SC[li // 2][:, (li % 2) * 256 + h * 64:(li % 2) * 256 + h * 64 + 64],
                                                lv, halves(lv, B)[:, :, 1 - key_half(dr)], start=True, stop=True)
                    if li % 2 == 1 or li == NL - 1:
                        last.then_inc(scores, 1)
                for h in range(H):
                    c = slice(h * P, (h + 1) * P)
                    last = nc.tensor.matmul(DG[:, c], qk[:, dr, k // 2, key_half(dr), c], qk[:, dr, k // 2, 1 - key_half(dr), c],
                                            start=True, stop=True)
                last.then_inc(scores, 1)
                fourier(i, k, part, 0)
                pe.wait_ge(ready, at(i, k, NL + 1, X + NL + 1))
                if isinstance(i, int) and i == 0 and k < 2:
                    pe.wait_ge(trcopy, X + k)
                else:
                    pe.wait_ge(o_out, at(i, k, 1, -1))
                transpose_keys(dr, k)
                fourier(i, k, part, 1)
                if not first:
                    pe.wait_ge(trcopy, at(i, k, 1, X + 1))
                    output(i, k - 1) if k else output(i - 1, SL - 1)
                if part == 2:
                    channels(i, k)
            run(pe, slot)
            pe.wait_ge(masked, NL * NU)
            pe.wait_ge(m64, NU)
            pe.wait_ge(o_out, NU - 1)
            output(NU // SL - 1, SL - 1)

        @block.scalar
        def _(act):
            def one_minus_f(dr, s):
                nc.scalar.activation(qk[:, dr, s, key_half(dr)], pre_of(dr, s), ACT.Identity, scale=-1.0, bias=g["one"][:, 0:1]
                                     ).then_inc(kk_done, 1)

            def keys_for(i, k):
                s, dr = k // 2, k % 2
                act.wait_ge(ld[dr][s], i * 48 + (32 * (NX // 2) + 48))
                one_minus_f(dr, s)

            def copy_keys(dr):
                nc.scalar.copy(kdT[:, dr], TO[:]).then_inc(trcopy, 1)

            def fourier(i, k, part, piece):
                if part == 1:
                    act.wait_ge(f_mm, at(i, k, 2, piece + 1))
                    if not (isinstance(i, int) and i == 0 and k < 2):
                        if piece == 0:
                            act.wait_ge(st_a[k % 2], i * 64 + 32 * (k // 2))
                    nc.scalar.copy(a_st[:, k % 2, piece, :], FT[:]).then_inc(f_out, 1)
                else:
                    act.wait_ge(f_mm, i * 12 + (F2 + 3 * k + piece + 1))
                    zv = zT[:, k % 2].rearrange("p r (t2 a b) -> p (r t2) a b", a=SL, b=8)
                    for x in range(2):
                        ins = nc.scalar.copy(zv[:, :, 2 * piece + x, :],
                                             FT[:, x * 256:(x + 1) * 256].rearrange("p (m b) -> p m b", b=8))
                    ins.then_inc(f_out, 1)

            def channels(i, k):
                act.wait_ge(f_mm, i * 12 + (F2 + 3 * k + 2 + 1))
                if k == 0:
                    act.wait_ge(st_f, i * 16 + (16 - 16 * 4))
                nc.scalar.copy(fst[:].rearrange("p (t2 x ab) -> p t2 x ab", x=SL, ab=32)[:, :, k, :],
                               FT[:].rearrange("p (t2 ab) -> p t2 ab", ab=32)).then_inc(f_out, 1)

            def output(i, k):
                act.wait_ge(o_mm, at(i, k, 1, 1))
                act.wait_ge(st_o[k % 2], i * 32 + 16 * (k // 2 + 1))
                nc.scalar.copy(ost[:, k % 2], TO[:]).then_inc(o_out, 1)

            act.sem_inc(f_out, 1)
            for n in range(X):
                act.wait_ge(ld[n % 2][n // 2 % 2], 32 * (n // 4 + 1))
                one_minus_f(n % 2, n // 2 % 2)
            for n in range(X):
                act.wait_ge(trans, n + 1)
                if n >= 2:
                    act.wait_ge(s_mm, n - 1)
                copy_keys(n % 2)
            keys_for(0, 0)
            keys_for(0, 1)

            def slot(i, k, part):
                dr = k % 2
                fourier(i, k, part, 0)
                act.wait_ge(trans, at(i, k, 1, X + 1))
                act.wait_ge(s_mm, at(i, k, 1, X - 1))
                copy_keys(dr)
                fourier(i, k, part, 1)
                if not (isinstance(i, int) and i == 0 and k == 0):
                    output(i, k - 1) if k else output(i - 1, SL - 1)
                act.wait_ge(masked, at(i, k, NL, NL))
                rows = slice(64 * key_half(dr), 64 * key_half(dr) + 64)
                q0 = 64 * (1 - key_half(dr))
                nc.scalar.copy(pm[rows, dr].rearrange("p (h t) -> p h t", h=H)[:, :, q0:q0 + 64],
                               SC[3][rows, 0:256].rearrange("p (h t) -> p h t", h=H)).then_inc(m64, 1)
                if part == 2:
                    channels(i, k)
                ni, nk = (i, k + 2) if k < 2 else (i + 1, k - 2)
                if not (isinstance(i, int) and i == NU // SL - 1 and k >= 2):
                    keys_for(ni, nk)
            run(act, slot)
            output(NU // SL - 1, SL - 1)

        @block.gpsimd
        def _(pool):
            def suf_ones(dr, s):
                nc.gpsimd.memset(w[:, dr, s, key_half(dr)], 1.0).then_inc(ones, 1)

            def store(i, k):
                s, dr = k // 2, k % 2
                pool.wait_ge(o_out, at(i, k, 1, 1))
                base = (P * s) if dr == 0 else ((NTT - 1 - s) * P)
                c = i * (2 * P if dr == 0 else -2 * P) + base
                cs = slice(c, c + P) if isinstance(c, int) else bass.ds(c, P)
                pool.dma_start(d["o"][dr][:, cs].rearrange("(h p) t -> p h t", p=P),
                               ost[:, dr].rearrange("p (h t) -> p h t", h=H)).then_inc(st_o[dr], 16)

            def load_x(i, k):
                gs = slice(P * (i - 4), P * (i - 3)) if isinstance(i, int) else bass.ds(i * P - 4 * P, P)
                for r in range(2):
                    pool.dma_start(xin[:, k % 2, r], ad.rearrange("n b r a c -> (n b) r a c")[:, r, SL * k:SL * k + SL, gs]
                                   ).then_inc(ld_x[k % 2], 16)

            prime(pool, d, g, st_o)
            prime(pool, d, g, [st_f])
            for n in range(X):
                suf_ones(n % 2, n // 2 % 2)
            for n in range(2):
                pool.wait_ge(s_new, n + 1)
                suf_ones(n % 2, 0)

            def slot(i, k, part):
                if part == 1:
                    pool.wait_ge(f_out, at(i, k, 2, 3))
                    n = slice(k, k + 1) if isinstance(i, int) else bass.ds(i * SL + k, 1)
                    for r in range(2):
                        pool.dma_start(ad[n, :, r].rearrange("n b a c -> (n a) b c"), a_st[:, k % 2, r, :]).then_inc(st_a[k % 2], 16)
                else:
                    if not (isinstance(i, int) and i == NU // SL - 1 and k == SL - 1):
                        pool.wait_ge(f_mm, i * 12 + (F2 + 3 * k - 1))
                        load_x(i, k + 1) if k < SL - 1 else load_x(i + 1, 0)
                if not (isinstance(i, int) and i == 0 and k == 0):
                    store(i, k - 1) if k else store(i - 1, SL - 1)
                if part == 2 and k == SL - 1:
                    pool.wait_ge(f_out, i * 12 + (F2 + 12 + 1))
                    rows = slice(P * (i - 4), P * (i - 3)) if isinstance(i, int) else bass.ds(i * P - 4 * P, P)
                    pool.dma_start(d["four"][rows, :], fst[:]).then_inc(st_f, 16)
                ni, nk = (i, k + 2) if k < 2 else (i + 1, k - 2)
                if not (isinstance(i, int) and i == NU // SL - 1 and k >= 2):
                    pool.wait_ge(s_new, at(ni, nk, 1, 1))
                    settle(pool, g)
                    suf_ones(nk % 2, nk // 2)

            for k in range(SL):
                slot(0, k, 1)
            with pool.Fori(1, 4) as i:
                for k in range(SL):
                    slot(i, k, 1)
            for s in range(2):
                pool.wait_ge(st_a[s], 16 * 16)
            load_x(4, 0)
            for k in range(SL):
                slot(4, k, 2)
            with pool.Fori(5, NU // SL - 1) as i:
                for k in range(SL):
                    slot(i, k, 2)
            for k in range(SL):
                slot(NU // SL - 1, k, 2)
            store(NU // SL - 1, SL - 1)
            for s in range(2):
                pool.wait_ge(st_o[s], 16 + 16 * NTT)
            pool.wait_ge(st_f, 16 + 16 * H)


def phase_merge(nc, d, g):
    NB = T // 512
    with Box(nc, "merge") as bx:
        raw = bx.sb("raw", [P, 2, D])
        wfh, wfl = bx.sb("wfh", [P, KB, D], F32R), bx.sb("wfl", [P, KB, D], F32R)
        wph, wpl = bx.sb("wph", [P, KB, D], F32R), bx.sb("wpl", [P, KB, D], F32R)
        four = bx.sb("four", [P, KB, 512])
        o2 = bx.sb("o2", [P, 2, KB, 512])
        og = bx.sb("og", [P, KB, 512])
        sq = bx.sb("sq", [P, KB, 512])
        fh, fl = bx.sb("fh", [P, 2, KB, 512], F32R), bx.sb("fl", [P, 2, KB, 512], F32R)
        oh, ol = bx.sb("oh", [P, 2, KB, 512], F32R), bx.sb("ol", [P, 2, KB, 512], F32R)
        gates = bx.sb("gates", [P, 2, 2, 512])
        t1 = bx.sb("t1", [P, 2, 512])
        y = bx.sb("y", [P, 2, 512])
        ng = bx.sb("ng", [P, KB])
        bank = bx.banks()
        ld_n, ld_w = bx.sem("ld_n"), [bx.sem(f"ld_w{i}") for i in range(2)]
        ld_o, ld_f, ld_og = bx.sem("ld_o"), bx.sem("ld_f"), bx.sem("ld_og")
        ld_g, st_y = [bx.sem(f"ld_g{i}") for i in range(2)], [bx.sem(f"st_y{i}") for i in range(2)]
        hi_s, lo_s, step_s, sum_s, sq_s, ms_s, rt_s, f_s, norm_s, og_s, o_s, mm_s, y_s = (bx.sem(n) for n in (
            "w_hi", "w_lo", "step", "o_sum", "o_sq", "ms_mm", "rms", "four_split", "o_normed", "og_used", "o_split", "mm", "y_done"))
        block = bx.block()

        @block.sync
        def _(sp):
            def load(sem, dst, src, b):
                sp.dma_start(dst, src[:, b * 512:(b + 1) * 512].rearrange("(h p) t -> p h t", p=P)).then_inc(sem, 16)

            def load_o(b):
                if b:
                    sp.wait_ge(norm_s, KB * b)
                for dr in range(2):
                    load(ld_o, o2[:, dr], d["o"][dr], b)

            def load_four(b):
                if b:
                    sp.wait_ge(f_s, b)
                load(ld_f, four[:], d["four"], b)

            def load_og(b):
                if b:
                    sp.wait_ge(og_s, b)
                load(ld_og, og[:], d["proj"][R_OG:R_OG + BR, :], b)

            def load_w(lo, hi):
                for n in range(lo, hi):
                    if n >= 2:
                        sp.wait_ge(lo_s, n - 1)
                    w = (d["w_four"], d["w_hgrn"])[n // KB]
                    sp.dma_start(raw[:, n % 2, :], w[(n % KB) * P:(n % KB + 1) * P, :]).then_inc(ld_w[n % 2], 16)
            sp.dma_start(ng[:], d["norm_g_col"]).then_inc(ld_n, 16)
            load_o(0)
            load_w(0, KB)
            load_four(0)
            load_og(0)
            load_w(KB, 2 * KB)
            for b in range(NB):
                for m in range(KD):
                    n = b * KD + m
                    if n >= 2:
                        sp.wait_ge(y_s, n - 1)
                    src = d["proj"][R_G:R_G + 2 * D, :].rearrange("(g m p) t -> m p g t", g=2, p=P)
                    sp.dma_start(gates[:, m % 2], src[m][:, :, b * 512:(b + 1) * 512]).then_inc(ld_g[m % 2], 16)
                    if m == 0 and b == 0:
                        load_o(1)
                    if m == 1 and b < NB - 1:
                        load_four(b + 1)
                    if m == 2 and b < NB - 1:
                        load_og(b + 1)
                    if m == 7 and b < NB - 2:
                        load_o(b + 2)

        @block.vector
        def _(dve):
            step = Count(step_s)

            def part_a(b):
                dve.wait_ge(ld_o, 32 * (b + 1))
                nc.vector.tensor_tensor(o2[:, 0], o2[:, 0], o2[:, 1], ALU.add).then_inc(sum_s, 1)

            def part_b(b):
                dve.wait_ge(ld_f, 16 * (b + 1))
                step.up(nc.vector.tensor_copy(fh[:, b % 2], four[:]))
                step.wait(dve)
                nc.vector.tensor_tensor(fl[:, b % 2], four[:], fh[:, b % 2].bitcast(F32), ALU.subtract).then_inc(f_s, 1)

            def part_c(b, h):
                dve.wait_ge(rt_s, KB * b + h + 1)
                step.up(nc.vector.reciprocal(o2[:, 1, h], o2[:, 1, h]))
                step.wait(dve)
                nc.vector.scalar_tensor_tensor(sq[:, h], o2[:, 0, h], ng[:, h:h + 1], o2[:, 1, h], ALU.mult, ALU.mult
                                               ).then_inc(norm_s, 1)

            def part_d(b):
                dve.wait_ge(ld_og, 16 * (b + 1))
                dve.wait_ge(norm_s, KB * (b + 1))
                nc.vector.tensor_tensor(sq[:], sq[:], og[:], ALU.mult).then_inc(og_s, 1)
                dve.wait_ge(og_s, b + 1)
                step.up(nc.vector.tensor_copy(oh[:, b % 2], sq[:]))
                step.wait(dve)
                nc.vector.tensor_tensor(ol[:, b % 2], sq[:], oh[:, b % 2].bitcast(F32), ALU.subtract).then_inc(o_s, 1)

            def gated(b, m):
                n = b * KD + m
                dve.wait_ge(ld_g[m % 2], 16 * (n // 2 + 1))
                dve.wait_ge(mm_s, n + 1)
                if n >= 2:
                    dve.wait_ge(y_s, n - 1)
                    dve.wait_ge(st_y[m % 2], 16 * (n // 2))
                pb = bank[2 * (n % 3):2 * (n % 3) + 2]
                step.up(nc.vector.tensor_tensor(t1[:, m % 2, :], gates[:, m % 2, 0, :], pb[0][:], ALU.mult))
                step.up(nc.vector.tensor_tensor(y[:, m % 2, :], gates[:, m % 2, 1, :], pb[1][:], ALU.mult))
                step.wait(dve)
                nc.vector.tensor_tensor(y[:, m % 2, :], y[:, m % 2, :], t1[:, m % 2, :], ALU.add).then_inc(y_s, 1)

            def weights(lo, hi):
                for n in range(lo, hi):
                    wh, wl = (wfh, wfl) if n < KB else (wph, wpl)
                    dve.wait_ge(hi_s, n + 1)
                    nc.vector.tensor_tensor(wl[:, n % KB, :], raw[:, n % 2, :], wh[:, n % KB, :].bitcast(F32), ALU.subtract
                                            ).then_inc(lo_s, 1)
            part_a(0)
            weights(0, KB)
            part_b(0)
            dve.wait_ge(ld_n, 16)
            for h in range(KB):
                part_c(0, h)
            part_d(0)
            weights(KB, 2 * KB)
            for b in range(NB):
                for m in range(KD):
                    gated(b, m)
                    if b == NB - 1:
                        continue
                    if m == 0:
                        part_a(b + 1)
                    elif m == 1:
                        part_b(b + 1)
                    elif m < 5:
                        for h in ((0, 1), (2,), (3,))[m - 2]:
                            part_c(b + 1, h)
                    elif m == 5:
                        part_d(b + 1)

        @block.scalar
        def _(act):
            def round_weights(lo, hi):
                for n in range(lo, hi):
                    act.wait_ge(ld_w[n % 2], 16 * (n // 2 + 1))
                    nc.scalar.copy((wfh if n < KB else wph)[:, n % KB, :], raw[:, n % 2, :]).then_inc(hi_s, 1)
            for b in range(NB):
                act.wait_ge(sum_s, b + 1)
                if b:
                    act.wait_ge(o_s, b)
                nc.scalar.activation(sq[:], o2[:, 0], ACT.Square).then_inc(sq_s, 1)
                if b == 0:
                    round_weights(0, KB)
                for h in range(KB):
                    act.wait_ge(ms_s, KB * b + h + 1)
                    nc.scalar.activation(o2[:, 1, h], bank[6 + h % 2][:], ACT.Sqrt, bias=g["eps"][:, 1:2]).then_inc(rt_s, 1)
                if b == 0:
                    round_weights(KB, 2 * KB)

        @block.tensor
        def _(pe):
            def mean_square(b):
                pe.wait_ge(sq_s, b + 1)
                for h in range(KB):
                    if KB * b + h >= 2:
                        pe.wait_ge(rt_s, KB * b + h - 1)
                    nc.tensor.matmul(bank[6 + h % 2][:], g["mean"][:], sq[:, h], start=True, stop=True).then_inc(ms_s, 1)
            def fourier(b, m):
                c = slice(m * P, (m + 1) * P)
                three_pass(nc, bank[2 * ((b * KD + m) % 3)][:], lambda k: (wfh[:, k, c], wfl[:, k, c]),
                           lambda k: (fh[:, b % 2, k], fl[:, b % 2, k]), KB)
            mean_square(0)
            pe.wait_ge(lo_s, KB)
            pe.wait_ge(f_s, 1)
            for m in range(3):
                fourier(0, m)
            pe.wait_ge(lo_s, 2 * KB)
            for b in range(NB):
                pe.wait_ge(f_s, b + 1)
                pe.wait_ge(o_s, b + 1)
                for m in range(KD):
                    n = b * KD + m
                    if n >= 3:
                        pe.wait_ge(y_s, n - 2)
                    c = slice(m * P, (m + 1) * P)
                    pb = bank[2 * (n % 3):2 * (n % 3) + 2]
                    if n >= 3:
                        fourier(b, m)
                    three_pass(nc, pb[1][:], lambda k: (wph[:, k, c], wpl[:, k, c]), lambda k: (oh[:, b % 2, k], ol[:, b % 2, k]), KB
                               ).then_inc(mm_s, 1)
                    if m == 1 and b < NB - 1:
                        mean_square(b + 1)

        @block.gpsimd
        def _(pool):
            for b in range(NB):
                for m in range(KD):
                    pool.wait_ge(y_s, b * KD + m + 1)
                    pool.dma_start(d["y"][m * P:(m + 1) * P, b * 512:(b + 1) * 512], y[:, m % 2, :]).then_inc(st_y[m % 2], 16)
            for s in range(2):
                pool.wait_ge(st_y[s], 16 * NB * KD // 2)


def layernorm_rows(nc, g, dve, step, r, stats, mv, mv_done, std_wait, std, rstd, out, sig):
    for c in range(2):
        step.up(nc.vector.bn_stats(stats[:, c, :], r[:, c * 512:(c + 1) * 512]))
    step.wait(dve)
    settle(dve, g)
    mv_done.up(nc.vector.bn_aggr(mv, stats.rearrange("p a b -> p (a b)")))
    mv_done.wait(dve)
    std_wait()
    step.up(nc.vector.reciprocal(rstd, std))
    step.wait(dve)
    sig.up(nc.vector.tensor_scalar(out, r, mv[:, 0:1], rstd, ALU.subtract, ALU.mult))


def phase_out_proj(nc, d, g):
    NB, W = T // 256, 256
    with Box(nc, "outp") as bx:
        raw = bx.sb("raw", [P, 2, D])
        wh, wl = bx.sb("wh", [P, KD, D], F32R), bx.sb("wl", [P, KD, D], F32R)
        y = bx.sb("y", [P, KD, W])
        yh, yl = bx.sb("yh", [P, 2, KD, W], F32R), bx.sb("yl", [P, 2, KD, W], F32R)
        xn = bx.sb("xn", [P, 2, D])
        r = bx.sb("r", [P, 2, D])
        xo = bx.sb("xo", [P, 2, D])
        ag, rb, tmp = bx.sb("ag", [P, D]), bx.sb("rb", [P, D]), bx.sb("tmp", [P, D])
        resv = bx.sb("resv", [1, 3, D])
        stats, mv, std, rstd = bx.sb("stats", [P, 2, 6]), bx.sb("mv", [P, 2]), bx.sb("std", [P, 1]), bx.sb("rstd", [P, 1])
        bank = bx.banks()
        ld_v, ld_w, ld_y = bx.sem("ld_v"), [bx.sem(f"ld_w{i}") for i in range(2)], bx.sem("ld_y")
        ld_x, st_x = [bx.sem(f"ld_x{i}") for i in range(2)], [bx.sem(f"st_x{i}") for i in range(2)]
        ld_r, st_r = bx.sem("ld_r"), bx.sem("st_r")
        sc_s, hi_s, lo_s, step_s, yh_s, yl_s, mm_s, rd_s, mv_s, std_s, xo_s = (bx.sem(n) for n in (
            "w_scaled", "w_hi", "w_lo", "step", "y_hi", "y_lo", "mm", "psum_read", "mv_done", "std", "xn1"))
        block = bx.block()

        @block.sync
        def _(sp):
            sp.dma_start(y[:], d["y"][:, 0:W].rearrange("(k p) t -> p k t", p=P)).then_inc(ld_y, 16)
            for n in range(KD):
                if n >= 2:
                    sp.wait_ge(lo_s, n - 1)
                sp.dma_start(raw[:, n % 2, :], d["w_out"][n * P:(n + 1) * P, :]).then_inc(ld_w[n % 2], 16)
                if n == 1:
                    for dst, src in ((ag, "ln_in_g"), (rb, "ln_in_b"), (tmp, "b_out")):
                        sp.dma_start(dst[:], d[src].partition_broadcast(P)).then_inc(ld_v, 16)
                    for k, src in enumerate(("g1", "b1p", "b_mlp2")):
                        sp.dma_start(resv[:, k, :], d[src].partition_broadcast(1)).then_inc(ld_r, 16)
            def rows(b):
                for t in range(2):
                    sp.wait_ge(rd_s, b * 4 + (2 * t + 6))
                    at = slice(t * P, (t + 1) * P) if isinstance(b, int) else bass.ds(b * W + t * P, P)
                    sp.dma_start(xn[:, t, :], d["xn"][at, :]).then_inc(ld_x[t], 16)
            rows(0)
            with sp.Fori(1, NB) as b:
                sp.wait_ge(yl_s, b + 1)
                sp.dma_start(y[:], d["y"][:, bass.ds(b * W, W)].rearrange("(k p) t -> p k t", p=P)).then_inc(ld_y, 16)
                rows(b)

        @block.vector
        def _(dve):
            step, rd, mvd, xo_c = Count(step_s), Count(rd_s, 8), Count(mv_s), Count(xo_s)
            dve.sem_inc(yl_s, 1)
            dve.sem_inc(rd_s, 8)
            def split(i, q):
                dve.wait_ge(ld_y, i * 32 + 16 * (q + 1))
                dve.wait_ge(mm_s, i * 8 + (4 * q + 4))
                nc.vector.tensor_copy(yh[:, q % 2], y[:]).then_inc(yh_s, 1)
                dve.wait_ge(yh_s, i * 2 + (q + 1))
                nc.vector.tensor_tensor(yl[:, q % 2], y[:], yh[:, q % 2].bitcast(F32), ALU.subtract).then_inc(yl_s, 1)

            def tile(i, q, t):
                dve.wait_ge(ld_x[t], i * 32 + 16 * (q + 1))
                step.up(nc.vector.tensor_tensor(xn[:, t, :], xn[:, t, :], ag[:], ALU.mult))
                step.wait(dve)
                step.up(nc.vector.tensor_tensor(xn[:, t, :], xn[:, t, :], rb[:], ALU.add))
                step.wait(dve)
                for c in range(2):
                    cs = slice(c * 512, (c + 1) * 512)
                    dve.wait_ge(mm_s, i * 8 + (8 + 4 * q + 2 * t + c + 1))
                    rd.up(nc.vector.tensor_tensor(r[:, t, cs], xn[:, t, cs], bank[2 * (2 * q + t) + c][:], ALU.add))
                rd.wait(dve)
                dve.wait_ge(st_x[t], i * 32 + 16 * (q + 1))
                layernorm_rows(nc, g, dve, step, r[:, t, :], stats[:], mv[:], mvd,
                               lambda: dve.wait_ge(std_s, i * 4 + (2 * q + t + 1)), std[:], rstd[:], xo[:, t, :], xo_c)
            split(0, 0)
            for k in range(KD):
                dve.wait_ge(ld_w[k % 2], 16 * (k // 2 + 1))
                nc.vector.tensor_tensor(raw[:, k % 2, :], raw[:, k % 2, :], g["mod2"][:], ALU.mult).then_inc(sc_s, 1)
                dve.wait_ge(sc_s, k + 1)
                nc.vector.tensor_copy(wh[:, k, :], raw[:, k % 2, :]).then_inc(hi_s, 1)
                dve.wait_ge(hi_s, k + 1)
                nc.vector.tensor_tensor(wl[:, k, :], raw[:, k % 2, :], wh[:, k, :].bitcast(F32), ALU.subtract).then_inc(lo_s, 1)
            dve.wait_ge(ld_v, 48)
            step.up(nc.vector.tensor_tensor(tmp[:], tmp[:], g["mod2"][:], ALU.mult))
            step.up(nc.vector.tensor_scalar(ag[:], ag[:], ALPHA, None, ALU.mult))
            step.wait(dve)
            step.up(nc.vector.scalar_tensor_tensor(rb[:], rb[:], ALPHA, tmp[:], ALU.mult, ALU.add))
            dve.wait_ge(ld_r, 48)
            step.up(nc.vector.tensor_tensor(resv[:, 2, :], resv[:, 2, :], g["mod5"][0:1, :], ALU.mult))
            step.up(nc.vector.tensor_scalar(resv[:, 0, :], resv[:, 0, :], ALPHA, None, ALU.mult))
            step.wait(dve)
            step.up(nc.vector.scalar_tensor_tensor(resv[:, 1, :], resv[:, 1, :], ALPHA, resv[:, 2, :], ALU.mult, ALU.add))
            step.wait(dve)
            with repeat(dve, 0, NB // 2 - 1, {step: 4 * 5, rd: 8, mvd: 4, xo_c: 4}) as i:
                for q in range(2):
                    split(i, q + 1)
                    for t in range(2):
                        tile(i, q, t)
            i = NB // 2 - 1
            split(i, 1)
            for q in range(2):
                for t in range(2):
                    tile(i, q, t)

        @block.scalar
        def _(act):
            with act.Fori(0, 2 * NB) as n:
                act.wait_ge(mv_s, n + 1)
                nc.scalar.activation(std[:], mv[:, 1:2], ACT.Sqrt, bias=g["eps"][:, 0:1]).then_inc(std_s, 1)

        @block.tensor
        def _(pe):
            pe.sem_inc(mm_s, 8)

            def blk(i, q):
                pe.wait_ge(yl_s, i * 2 + (q + 2))
                for t in range(2):
                    for c in range(2):
                        n = 4 * q + 2 * t + c
                        pe.wait_ge(rd_s, i * 8 + (n + 1))
                        ts, cs = slice(t * P, (t + 1) * P), slice(c * 512, (c + 1) * 512)
                        three_pass(nc, bank[n][:], lambda k: (yh[:, q, k, ts], yl[:, q, k, ts]),
                                   lambda k: (wh[:, k, cs], wl[:, k, cs]), KD).then_inc(mm_s, 1)
            pe.wait_ge(yl_s, 2)
            for k in range(KD):
                pe.wait_ge(lo_s, k + 1)
                for n in range(4):
                    ts, cs = slice(n // 2 * P, (n // 2 + 1) * P), slice(n % 2 * 512, (n % 2 + 1) * 512)
                    nc.tensor.matmul(bank[n][:], yh[:, 0, k, ts], wh[:, k, cs], start=(k == 0), stop=False)
                    nc.tensor.matmul(bank[n][:], yh[:, 0, k, ts], wl[:, k, cs], start=False, stop=False)
                    last = nc.tensor.matmul(bank[n][:], yl[:, 0, k, ts], wh[:, k, cs], start=False, stop=(k == KD - 1))
                    if k == KD - 1:
                        last.then_inc(mm_s, 1)
            blk(0, 1)
            with pe.Fori(1, NB // 2) as i:
                for q in range(2):
                    blk(i, q)

        @block.gpsimd
        def _(pool):
            prime(pool, d, g, st_x)
            pool.wait_ge(step_s, 6)
            pool.dma_start(d["res"].rearrange("(o r) n -> o r n", o=1), resv[:, 0:2, :]).then_inc(st_r, 16)
            with pool.Fori(0, NB) as b:
                for t in range(2):
                    pool.wait_ge(xo_s, b * 2 + (t + 1))
                    pool.dma_start(d["xn1"][bass.ds(b * W + t * P, P), :], xo[:, t, :]).then_inc(st_x[t], 16)
            pool.wait_ge(st_r, 16)
            for s in range(2):
                pool.wait_ge(st_x[s], 16 + 16 * NB)


def phase_mlp(nc, d, g, half):
    NP_ = FF // P // 2
    NT, HW = KD, T // 2
    row0 = half * HW
    with Box(nc, f"mlp{half}") as bx:
        acc = bx.sb("acc", [P, NT, D])
        hT = (bx.sb("h2h", [P, KD, HW], F32R), bx.sb("h2l", [P, KD, HW], F32R))
        stats, mv, std, rstd = (bx.sb("stats", [P, 2, 2, 6]), bx.sb("mv", [P, NT, 2]), bx.sb("std", [P, NT]),
                                bx.sb("rstd", [P, NT]))
        raw1 = bx.sb("raw1", [P, 2, KD, P])
        w1h, w1l = bx.sb("w1h", [P, 2, KD, P], F32R), bx.sb("w1l", [P, 2, KD, P], F32R)
        raw2 = bx.sb("raw2", [P, 2, D])
        w2h, w2l = bx.sb("w2h", [P, 4, D], F32R), bx.sb("w2l", [P, 4, D], F32R)
        ah, al = bx.sb("ah", [P, 4, D], F32R), bx.sb("al", [P, 4, D], F32R)
        a = bx.sb("a", [P, 2, 512])
        b1 = bx.sb("b1", [P, FF // P])
        res = g["mod2"][:].rearrange("p (two one n) -> p two one n", two=2, one=1)
        tail = raw1[:].rearrange("p s k n -> p s (k n)")
        bank = bx.banks()
        U, V = bank[0:4], bank[4:8]
        ld_b = bx.sem("ld_b")
        ld_1, ld_2 = [bx.sem(f"ld_1{i}") for i in range(2)], [bx.sem(f"ld_2{i}") for i in range(2)]
        w1hi, w1lo, w2hi, w2lo, up_s, relu_s, sq_s, ahi_s, al_s, dn_s, acc_s = (bx.sem(n) for n in (
            "w1_hi", "w1_lo", "w2_hi", "w2_lo", "up", "relu", "sq", "a_hi", "a_lo", "down", "acc"))
        ld_a, ld_t = [bx.sem(f"ld_a{i}") for i in range(2)], bx.sem("ld_t")
        ld_v, st_x = [bx.sem(f"st_v{i}") for i in range(2)], bx.sem("st_x")
        xT, evac, h_hi, split, w2s, step_s, mv_s, std_s, out_s = (bx.sem(n) for n in (
            "xT", "evac", "h_hi", "h_split", "w2_scaled", "step", "mv_done", "std", "out"))
        block = bx.block()

        def peeled(eng, body):
            body(0, 'u', 0)
            with eng.Fori(0, NP_ // 2 - 1) as i:
                for x, qn in (('u', 1), ('d', 0), ('u', 2), ('d', 1)):
                    body(i, x, qn)
            for x, qn in (('u', NP_ - 1), ('d', NP_ - 2), ('d', NP_ - 1)):
                body(0, x, qn)

        def load_rows(eng, gi):
            rows = d["xn1"][row0 + gi * 512:row0 + (gi + 1) * 512, :].rearrange("(s p) n -> p s n", p=P)
            eng.dma_start(acc[:, 4 * gi:4 * gi + 4], rows).then_inc(ld_a[gi], 16)

        @block.sync
        def _(sp):
            load_rows(sp, 0)
            sp.dma_start(b1[:], d["b1_col"]).then_inc(ld_b, 16)
            with sp.Fori(0, NP_) as p:
                for e in range(2):
                    sp.wait_ge(w1lo, p * 2 + (e + 1))
                    sp.dma_start(raw1[:, e], d["w1"][:, bass.ds(p * 2 * P + e * P, P)].rearrange("(k p) n -> p k n", p=P)
                                 ).then_inc(ld_1[e], 16)
                    sp.wait_ge(w2lo, p * 2 + (e + 1))
                    sp.dma_start(raw2[:, e, :], d["w2"][bass.ds(p * 2 * P + e * P, P), :]).then_inc(ld_2[e], 16)
            sp.wait_ge(w1lo, 2 * NP_ + 2)
            for n, src in enumerate(("g2", "b2p")):
                sp.dma_start(tail[:, n], d[src].partition_broadcast(P)).then_inc(ld_t, 16)

        @block.vector
        def _(dve):
            dve.sem_inc(w1lo, 2)
            dve.sem_inc(w2lo, 2)
            dve.sem_inc(acc_s, 4)
            dve.sem_inc(al_s, 2)
            dve.sem_inc(split, 2)
            step = Count(step_s)

            def split_h(gi):
                for k in range(KD):
                    n, cs = gi * KD + k, slice(gi * 512, (gi + 1) * 512)
                    dve.wait_ge(evac, n + 1)
                    nc.vector.tensor_copy(hT[0][:, k, cs], a[:, k % 2, :]).then_inc(h_hi, 1)
                    dve.wait_ge(h_hi, n + 1)
                    nc.vector.tensor_tensor(hT[1][:, k, cs], a[:, k % 2, :], hT[0][:, k, cs].bitcast(F32), ALU.subtract
                                            ).then_inc(split, 1)

            def residual(c):
                half_rows = acc[:, :, c * 512:(c + 1) * 512]
                dve.wait_ge(ld_v[c], 32)
                step.up(nc.vector.tensor_tensor(half_rows, half_rows, res[:, 0].to_broadcast([P, NT, 512]), ALU.mult))
                step.wait(dve)
                step.up(nc.vector.tensor_tensor(half_rows, half_rows, res[:, 1].to_broadcast([P, NT, 512]), ALU.add))
                step.wait(dve)

            def gather_rows():
                q = NP_ - 1
                dve.wait_ge(ld_t, 32)

                def result(t):
                    dve.wait_ge(std_s, t + 1)
                    step.up(nc.vector.reciprocal(rstd[:, t:t + 1], std[:, t:t + 1]))
                    step.up(nc.vector.scalar_tensor_tensor(acc[:, t], acc[:, t], mv[:, t, 0:1], tail[:, 0], ALU.subtract, ALU.mult))
                    step.wait(dve)
                    nc.vector.scalar_tensor_tensor(acc[:, t], acc[:, t], rstd[:, t:t + 1], tail[:, 1], ALU.mult, ALU.add
                                                   ).then_inc(out_s, 1)
                for t in range(NT):
                    for c in range(2):
                        n, dst = 2 * t + c, acc[:, t, c * 512:(c + 1) * 512]
                        dve.wait_ge(dn_s, 16 * q + n + 1)
                        nc.vector.tensor_tensor(dst, dst, V[n % 4][:], ALU.add).then_inc(acc_s, 1)
                    dve.wait_ge(acc_s, 16 * q + 2 * t + 2 + 4)
                    for c in range(2):
                        step.up(nc.vector.bn_stats(stats[:, t % 2, c, :], acc[:, t, c * 512:(c + 1) * 512]))
                    if t:
                        result(t - 1)
                    step.wait(dve)
                    nc.vector.bn_aggr(mv[:, t, :], stats[:, t % 2].rearrange("p a b -> p (a b)")).then_inc(mv_s, 1)
                result(NT - 1)

            def split1(i, q, strips=(0, 1)):
                for e in strips:
                    dve.wait_ge(ld_1[e], i * 32 + 16 * (q + 1))
                    if isinstance(i, int) and q == 0:
                        pass
                    else:
                        dve.wait_ge(up_s, i * 8 + (4 * q - 4 + 2 * e + 2))
                    nc.vector.tensor_copy(w1h[:, e], raw1[:, e]).then_inc(w1hi, 1)
                    dve.wait_ge(w1hi, i * 4 + (2 * q + e + 1))
                    nc.vector.tensor_tensor(w1l[:, e], raw1[:, e], w1h[:, e].bitcast(F32), ALU.subtract).then_inc(w1lo, 1)

            def split2(i, q):
                for e in range(2):
                    z = 2 * (q % 2) + e
                    dve.wait_ge(ld_2[e], i * 32 + 16 * (q + 1))
                    nc.vector.tensor_tensor(raw2[:, e], raw2[:, e], g["mod5"][:], ALU.mult).then_inc(w2s, 1)
                    dve.wait_ge(w2s, i * 4 + (2 * q + e + 1))
                    nc.vector.tensor_copy(w2h[:, z], raw2[:, e]).then_inc(w2hi, 1)
                    dve.wait_ge(w2hi, i * 4 + (2 * q + e + 1))
                    nc.vector.tensor_tensor(w2l[:, z], raw2[:, e], w2h[:, z].bitcast(F32), ALU.subtract).then_inc(w2lo, 1)

            def hidden(i, q, strips=(0, 1)):
                for e in strips:
                    for c in range(2):
                        z, cs = 2 * (q % 2) + e, slice(c * 512, (c + 1) * 512)
                        n = 4 * q + 2 * e + c
                        dve.wait_ge(sq_s, i * 8 + (n + 1))
                        nc.vector.tensor_copy(ah[:, z, cs], a[:, c, :]).then_inc(ahi_s, 1)
                        dve.wait_ge(ahi_s, i * 8 + (n + 1))
                        nc.vector.tensor_tensor(al[:, z, cs], a[:, c, :], ah[:, z, cs].bitcast(F32), ALU.subtract).then_inc(al_s, 1)

            def gather(i, q):
                for n in range(16):
                    dve.wait_ge(dn_s, i * 32 + (16 * q + n + 1))
                    t, c = n // 2, n % 2
                    dst = acc[:, t, c * 512:(c + 1) * 512]
                    nc.vector.tensor_tensor(dst, dst, V[n % 4][:], ALU.add).then_inc(acc_s, 1)
                    if n in (5, 9) and not (isinstance(i, int) and q == NP_ - 2):
                        split1(i, q + 2, (n // 9,))

            def body(i, x, q):
                if x == 'u' and isinstance(i, int) and q == 0:
                    residual(0)
                    for e in range(2):
                        hidden(0, 0, (e,))
                        split1(0, 1, (e,))
                    residual(1)
                    split2(0, 1)
                elif x == 'u':
                    hidden(i, q)
                elif isinstance(i, int) and q == NP_ - 1:
                    gather_rows()
                else:
                    gather(i, q)
                    if not (isinstance(i, int) and q >= NP_ - 2):
                        split2(i, q + 2)
            split_h(0)
            split1(0, 0)
            split_h(1)
            split2(0, 0)
            peeled(dve, body)

        @block.scalar
        def _(act):
            load_rows(act, 1)
            for n in range(2 * KD):
                k = n % KD
                act.wait_ge(xT, n + 1)
                act.wait_ge(split, n + 1)
                nc.scalar.activation(a[:, k % 2, :], bank[k][:], ACT.Identity, bias=g["shift"][:, 2, k:k + 1],
                                     scale=g["scale"][:, 2, k:k + 1]).then_inc(evac, 1)
            act.wait_ge(split, 2 * KD + 2)
            act.wait_ge(ld_b, 16)

            def body(i, x, q):
                if x == 'd':
                    return
                for e in range(2):
                    for c in range(2):
                        n = 4 * q + 2 * e + c
                        act.wait_ge(up_s, i * 8 + (n + 1))
                        act.wait_ge(al_s, i * 8 + (n + 1))
                        col = 2 * q + e
                        bias = b1[:, col:col + 1] if isinstance(i, int) else b1[:, bass.ds(i * 4 + col, 1)]
                        settle(act, g)
                        nc.scalar.activation(a[:, c, :], U[2 * e + c][:], ACT.Relu, bias=bias).then_inc(relu_s, 1)
                        act.wait_ge(relu_s, i * 8 + (n + 1))
                        nc.scalar.activation(a[:, c, :], a[:, c, :], ACT.Square).then_inc(sq_s, 1)
            peeled(act, body)
            for t in range(NT):
                act.wait_ge(mv_s, t + 1)
                nc.scalar.activation(std[:, t:t + 1], mv[:, t, 1:2], ACT.Sqrt, bias=g["eps"][:, 0:1]).then_inc(std_s, 1)

        @block.tensor
        def _(pe):
            for n in range(2 * KD):
                k, gi = n % KD, n // KD
                pe.wait_ge(ld_a[gi], 16)
                if gi:
                    pe.wait_ge(evac, k + 1)
                for s in range(4):
                    last = nc.tensor.transpose(bank[k][:, s * P:(s + 1) * P], acc[:, 4 * gi + s, k * P:(k + 1) * P], g["ident"][:])
                last.then_inc(xT, 1)
            pe.wait_ge(evac, 2 * KD)

            def body(i, x, q):
                if x == 'u':
                    for e in range(2):
                        pe.wait_ge(w1lo, i * 4 + (2 * q + e + 1 + 2))
                        for c in range(2):
                            n = 4 * q + 2 * e + c
                            if not (isinstance(i, int) and q == 0):
                                pe.wait_ge(relu_s, i * 8 + (n - 3))
                            else:
                                pe.wait_ge(split, KD * (c + 1) + 2)
                            cs = slice(c * 512, (c + 1) * 512)
                            three_pass(nc, U[2 * e + c][:], lambda k: (w1h[:, e, k, :], w1l[:, e, k, :]),
                                       lambda k: (hT[0][:, k, cs], hT[1][:, k, cs]), KD).then_inc(up_s, 1)
                else:
                    pe.wait_ge(al_s, i * 8 + (4 * q + 4 + 2))
                    pe.wait_ge(w2lo, i * 4 + (2 * q + 2 + 2))
                    for n in range(16):
                        t, c = n // 2, n % 2
                        pe.wait_ge(acc_s, i * 32 + (16 * q + n + 1))
                        ts, cs = slice(t * P, (t + 1) * P), slice(c * 512, (c + 1) * 512)
                        z = 2 * (q % 2)
                        three_pass(nc, V[n % 4][:], lambda k: (ah[:, z + k, ts], al[:, z + k, ts]),
                                   lambda k: (w2h[:, z + k, cs], w2l[:, z + k, cs]), 2).then_inc(dn_s, 1)
            peeled(pe, body)

        @block.gpsimd
        def _(pool):
            for c in range(2):
                if c:
                    pool.wait_ge(step_s, 2)
                for r in range(2):
                    pool.dma_start(res[:, r, 0, :], d["res"][r, c * 512:(c + 1) * 512].partition_broadcast(P)).then_inc(ld_v[c], 16)
            for t in range(NT):
                pool.wait_ge(out_s, t + 1)
                pool.dma_start(d["out"][row0 + t * P:row0 + (t + 1) * P, :], acc[:, t]).then_inc(st_x, 16)
            pool.wait_ge(st_x, 16 * NT)


def build_program(nc, d):
    def scratch(name, shape):
        d[name] = nc.dram_tensor(f"scratch_{name}", shape, F32, kind="Internal").ap()

    scratch("pad", (24, 1, 16))
    scratch("xn", (T, D))
    scratch("xn1", (T, D))
    scratch("res", (2, D))
    scratch("proj", (R_G + 2 * D, T))
    scratch("proj_ctx", (2 * BR, TC))
    scratch("u", (NTT, P, BR))
    scratch("v", (T, BR))
    scratch("v_ctx", (TC, BR))
    scratch("dft_a", (NTT, 8, 2, NTT, BR))
    scratch("four", (BR, T))
    scratch("o", (2, BR, T))
    scratch("y", (D, T))

    with Box(nc, "all") as bx:
        g = {
            "ident": bx.sb("ident", [P, P]),
            "mean": bx.sb("mean", [P, P]),
            "eps": bx.sb("eps", [P, 2]),
            "one": bx.sb("one", [P, 1]),
            "scale": bx.sb("scale", [P, 3, KD]),
            "shift": bx.sb("shift", [P, 3, KD]),
            "lb": bx.sb("lb", [P, 2, H]),
            "oml": bx.sb("oml", [P, 2, H]),
            "b_in_col": bx.sb("b_in_col", [P, 40]),
            "mod2": bx.sb("mod2", [P, D]),
            "mod5": bx.sb("mod5", [P, D]),
            "primed": 0,
            "settled": bx.sem("settled"),
        }
        with Box(nc, "const") as cx:
            ld = cx.sem("ld")
            block = cx.block()

            @block.sync
            def _(sp):
                sp.dma_start(g["ident"][:], d["ident"]).then_inc(ld, 16)
                sp.dma_start(g["b_in_col"][:], d["b_in_col"]).then_inc(ld, 16)
                sp.wait_ge(ld, 32)

            @block.vector
            def _(dve):
                nc.vector.memset(g["mean"][:], 1.0 / P)
                nc.vector.memset(g["eps"][:, 0:1], LN_EPS)
                nc.vector.memset(g["one"][:], 1.0)
                nc.vector.memset(g["eps"][:, 1:2], RMS_EPS)
        with Box(nc, "act") as ax:
            hT = (ax.sb("hTh", [P, KD, T], F32R), ax.sb("hTl", [P, KD, T], F32R))
            cT = (ax.sb("cTh", [P, KD, TC], F32R), ax.sb("cTl", [P, KD, TC], F32R))
            phase_front(nc, d, g, hT, cT)
            phase_project(nc, d, g, hT, cT)
            phase_project_tokens(nc, d, g, hT, cT)
        phase_mix(nc, d, g)
        phase_merge(nc, d, g)
        phase_out_proj(nc, d, g)
        for half in range(2):
            phase_mlp(nc, d, g, half)


def shape_constants():
    c = {"ident": np.eye(P, dtype=np.float32)}
    quarter = D // 4
    omega = (1.0 / (np.float32(10000.0) ** (np.arange(quarter, dtype=np.float32) / np.float32(quarter)))).astype(np.float32)
    r = np.arange(T // GRID_W, dtype=np.float32)[:, None] * omega
    w = np.arange(GRID_W, dtype=np.float32)[:, None] * omega
    c["pos_row"] = np.concatenate([np.sin(r), np.cos(r)], -1).astype(np.float32)
    ec = np.concatenate([np.sin(w), np.cos(w)], -1).astype(np.float32)
    c["pos_col"] = np.concatenate([ec, ec], 0)
    n1, n2, t1 = np.arange(P), np.arange(NTT), np.arange(P)
    ph = 2 * np.pi * ((t1[None, None, :] * (NTT * n1[None, :, None] + n2[:, None, None])) % T) / T
    c["dft_m1"] = np.stack([np.cos(ph), -np.sin(ph)], 2).astype(np.float32)
    p16 = 2 * np.pi * ((n2[:, None] * n2[None, :]) % NTT) / NTT
    eye8 = np.eye(8)
    bc, bs = np.kron(np.cos(p16), eye8), np.kron(np.sin(p16), eye8)
    c["dft_m2"] = np.stack([np.concatenate([bc, -bs], 1), np.concatenate([bs, bc], 1)], 1).astype(np.float32)
    pg = 2 * np.pi * ((n1[:, None] * n1[None, :]) % P) / P
    c["dft_m3"] = (np.stack([np.cos(pg), np.sin(pg)], 1) / np.sqrt(T * P)).astype(np.float32)
    m = np.zeros((P, 2, NL - 1, H, 64), np.int32)
    s = np.arange(P)[:, None]
    t = np.arange(P)[None, :]
    for li, B in enumerate(LEVELS[:-1]):
        for dr in range(2):
            later = (t // B) % 2 == 1 - dr
            ok = (s // (2 * B) == t // (2 * B)) & later & ((s // B) % 2 == dr)
            cols = np.nonzero(later[0])[0]
            m[:, dr, li] = ok[:, cols][:, None, :]
    c["masks"] = m.reshape(P, 2, NL - 1, 256)
    c["diag"] = np.tile(np.eye(P, dtype=np.int32), (1, H))
    return c


def columns(v):
    v = np.asarray(v)
    return np.ascontiguousarray(v.reshape(v.shape[:-1] + (-1, P)).swapaxes(-1, -2))


def kernel(x, c, ctx, c_ctx, ln_in_g, ln_in_b, w_ada, b_ada, w_in, b_in, hgrn_lb_logits, hgrn_norm_g,
           w_four_proj, w_hgrn_proj, w_out, b_out, w_mlp1, b_mlp1, w_mlp2, b_mlp2, ln_post_g, ln_post_b):
    import concourse.bacc as bacc
    from concourse.bass_utils import run_bass_kernel_spmd

    A = np.asarray
    arrays = {
        "x": A(x)[0], "ctx": A(ctx)[0],
        "ccol": np.ascontiguousarray(np.stack([columns(A(c)[0]), columns(A(c_ctx))], -1)),
        "ln_in_g": A(ln_in_g), "ln_in_b": A(ln_in_b),
        "ln_cols": np.ascontiguousarray(np.stack([columns(A(ln_in_g)), columns(A(ln_in_b)), columns(A(ln_post_g)[0, 0]),
                                                  columns(A(ln_post_b)[0, 0])], 1)),
        "w_ada": A(w_ada)[0], "b_ada": A(b_ada)[0], "b_ada_col": columns(A(b_ada)[0]),
        "w_in": A(w_in)[0], "b_in": A(b_in)[0], "b_in_col": columns(A(b_in)[0]),
        "lb_logits": np.ascontiguousarray(A(hgrn_lb_logits).reshape(2, 2, H, P).transpose(3, 0, 1, 2)),
        "norm_g_col": columns(A(hgrn_norm_g)[0]),
        "w_four": A(w_four_proj)[0], "w_hgrn": A(w_hgrn_proj)[0], "w_out": A(w_out)[0], "b_out": A(b_out)[0],
        "w1": A(w_mlp1)[0], "b1_col": columns(A(b_mlp1)[0]), "w2": A(w_mlp2)[0], "b_mlp2": A(b_mlp2)[0],
        "g1": A(ln_post_g)[0, 0], "b1p": A(ln_post_b)[0, 0], "g2": A(ln_post_g)[0, 1], "b2p": A(ln_post_b)[0, 1],
    }
    arrays.update(shape_constants())
    nc = bacc.Bacc("TRN2", target_bir_lowering=False, num_devices=1)
    sent, d = {}, {}
    for name, a in arrays.items():
        a = np.ascontiguousarray(a)
        sent[f"in_{name}"] = a
        d[name] = nc.dram_tensor(f"in_{name}", a.shape, mybir.dt.from_np(a.dtype), kind="ExternalInput").ap()
    d["out"] = nc.dram_tensor("out_x", (T, D), F32, kind="ExternalOutput").ap()
    build_program(nc, d)
    r = run_bass_kernel_spmd(nc, [sent], core_ids=[0])
    return r.results[0]["out_x"].reshape(1, T, D)
```
